# Optimizing a Trainium2 kernel written in Bass

```python
import jax, jax.numpy as jnp
from jax import lax
import numpy as np

D_MODEL = 1024
BATCH = 1
SEQ = 256
DEPTH = 2

N_MIXERS = 2
N_A_LAYERS = (DEPTH + 1) // 2
N_B_LAYERS = DEPTH // 2
EPS = 1e-6

D_FF = ((8 * D_MODEL // 3 + 127) // 128) * 128

A_DK = 128
A_DV = 128
A_HEADS = D_MODEL // A_DK
A_CONV = 4
A_CHUNK = 64

B_HD = 64
B_HEADS = D_MODEL // B_HD
B_KV_HEADS = 4
B_WINDOW = 128
B_BLOCK = 128


def rmsnorm(x, w):
    xf = x.astype(jnp.float32)
    y = xf * lax.rsqrt(jnp.mean(xf * xf, axis=-1, keepdims=True) + EPS) * w.astype(jnp.float32)
    return y.astype(x.dtype)

def l2norm(x):
    xf = x.astype(jnp.float32)
    return xf * lax.rsqrt(jnp.sum(xf * xf, axis=-1, keepdims=True) + EPS)

def swiglu(h, w_gu, w_down):
    gate, up = jnp.split(h @ w_gu, 2, axis=-1)
    return (jax.nn.silu(gate) * up) @ w_down

def causal_depthwise_conv(x, w):
    C = x.shape[-1]
    return lax.conv_general_dilated(
        x, w[:, None, :].astype(x.dtype), window_strides=(1,), padding=[(A_CONV - 1, 0)],
        dimension_numbers=("NWC", "WIO", "NWC"), feature_group_count=C)

def gated_delta_rule_chunked(q, k, v, g, beta):
    Bsz, T, H, DK = q.shape
    DV = v.shape[-1]
    C = A_CHUNK
    N = T // C
    f32 = jnp.float32

    def chunk(t):
        return t.astype(f32).reshape(Bsz, N, C, H, -1).transpose(0, 3, 1, 2, 4)

    q, k, v = chunk(q), chunk(k), chunk(v)
    g = g.astype(f32).reshape(Bsz, N, C, H).transpose(0, 3, 1, 2)
    beta = beta.astype(f32).reshape(Bsz, N, C, H).transpose(0, 3, 1, 2)
    g = jnp.cumsum(g, axis=-1)

    idx = jnp.arange(C)
    lower_incl = idx[:, None] >= idx[None, :]
    strict = idx[:, None] > idx[None, :]
    decay = jnp.exp(jnp.where(lower_incl, g[..., :, None] - g[..., None, :], -jnp.inf))

    kb = k * beta[..., None]
    L = jnp.where(strict, jnp.einsum("bhnid,bhnjd->bhnij", kb, k) * decay, 0.0)
    rhs = jnp.concatenate([v * beta[..., None], kb * jnp.exp(g)[..., None]], axis=-1)
    sol = lax.linalg.triangular_solve(L, rhs, left_side=True, lower=True,
                                      transpose_a=False, conjugate_a=False, unit_diagonal=True)
    u, w = sol[..., :DV], sol[..., DV:]

    a_qk = jnp.einsum("bhnid,bhnjd->bhnij", q, k) * decay
    q_dec = q * jnp.exp(g)[..., None]
    k_dec = k * jnp.exp(g[..., -1:] - g)[..., None]
    g_last = jnp.exp(g[..., -1])

    xs = (jnp.moveaxis(q_dec, 2, 0), jnp.moveaxis(k_dec, 2, 0), jnp.moveaxis(u, 2, 0),
          jnp.moveaxis(w, 2, 0), jnp.moveaxis(a_qk, 2, 0), jnp.moveaxis(g_last, 2, 0))

    def step(S, inp):
        qd, kd, u_c, w_c, a_c, gl = inp
        v_new = u_c - jnp.einsum("bhck,bhkv->bhcv", w_c, S)
        o = jnp.einsum("bhck,bhkv->bhcv", qd, S) + jnp.einsum("bhij,bhjv->bhiv", a_c, v_new)
        S = S * gl[..., None, None] + jnp.einsum("bhck,bhcv->bhkv", kd, v_new)
        return S, o

    S0 = jnp.zeros((Bsz, H, DK, DV), f32)
    _, o = lax.scan(step, S0, xs)
    return o.transpose(1, 0, 3, 2, 4).reshape(Bsz, T, H, DV)

def mixer_gated_deltanet(h, w_in, w_conv, A_log, dt_bias, out_norm, w_out):
    Bsz, T, _ = h.shape
    HK = A_HEADS * A_DK
    HV = A_HEADS * A_DV
    proj = h @ w_in
    qkv = proj[..., :2 * HK + HV]
    z = proj[..., 2 * HK + HV:2 * HK + 2 * HV]
    b = proj[..., 2 * HK + 2 * HV:2 * HK + 2 * HV + A_HEADS]
    a = proj[..., 2 * HK + 2 * HV + A_HEADS:]
    qkv = jax.nn.silu(causal_depthwise_conv(qkv, w_conv))
    q = l2norm(qkv[..., :HK].reshape(Bsz, T, A_HEADS, A_DK)) * (A_DK ** -0.5)
    k = l2norm(qkv[..., HK:2 * HK].reshape(Bsz, T, A_HEADS, A_DK))
    v = qkv[..., 2 * HK:].reshape(Bsz, T, A_HEADS, A_DV)
    beta = jax.nn.sigmoid(b.astype(jnp.float32))
    g = -jnp.exp(A_log.astype(jnp.float32)) * jax.nn.softplus(a.astype(jnp.float32) + dt_bias.astype(jnp.float32))
    o = gated_delta_rule_chunked(q, k, v, g, beta)
    zf = z.reshape(Bsz, T, A_HEADS, A_DV).astype(jnp.float32)
    o = rmsnorm(o, out_norm) * jax.nn.silu(zf)
    return o.reshape(Bsz, T, HV).astype(h.dtype) @ w_out

def mixer_sliding_window_sinks(h, w_in, b_in, sinks, w_out, b_out):
    Bsz, T, _ = h.shape
    G = B_HEADS // B_KV_HEADS
    NB = T // B_BLOCK
    HQ = B_HEADS * B_HD
    HKV = B_KV_HEADS * B_HD
    proj = h @ w_in + b_in
    q = proj[..., :HQ].reshape(Bsz, NB, B_BLOCK, B_KV_HEADS, G, B_HD)
    k = proj[..., HQ:HQ + HKV].reshape(Bsz, NB, B_BLOCK, B_KV_HEADS, B_HD)
    v = proj[..., HQ + HKV:].reshape(Bsz, NB, B_BLOCK, B_KV_HEADS, B_HD)

    def with_prev(t):
        prev = jnp.concatenate([jnp.zeros_like(t[:, :1]), t[:, :-1]], axis=1)
        return jnp.concatenate([prev, t], axis=2)

    kk, vv = with_prev(k), with_prev(v)
    s = jnp.einsum("bnqhgd,bnkhd->bnhgqk", q, kk).astype(jnp.float32) * (B_HD ** -0.5)
    qi = jnp.arange(B_BLOCK)[:, None]
    kj = jnp.arange(2 * B_BLOCK)[None, :]
    rel = qi + B_BLOCK - kj
    band = (rel >= 0) & (rel < B_WINDOW)
    blk = jnp.arange(NB)[:, None, None]
    valid = band[None] & ((blk > 0) | (kj >= B_BLOCK)[None])
    s = jnp.where(valid[None, :, None, None], s, -jnp.inf)
    sink = jnp.broadcast_to(sinks.astype(jnp.float32).reshape(B_KV_HEADS, G)[None, None, :, :, None, None],
                            s.shape[:-1] + (1,))
    p = jax.nn.softmax(jnp.concatenate([s, sink], axis=-1), axis=-1)[..., :-1]
    o = jnp.einsum("bnhgqk,bnkhd->bnqhgd", p.astype(vv.dtype), vv)
    return o.reshape(Bsz, T, HQ) @ w_out + b_out

def first_inputs(seed: int = 0) -> dict:
    key = jax.random.key(seed)
    ks = iter(jax.random.split(key, 32))
    f32 = jnp.float32
    nrm = lambda shape, scale: jax.random.normal(next(ks), shape, f32) * scale
    gain = lambda shape: 1.0 + 0.02 * jax.random.normal(next(ks), shape, f32)
    D = D_MODEL
    a_in_cols = 2 * A_HEADS * A_DK + 2 * A_HEADS * A_DV + 2 * A_HEADS
    b_in_cols = (B_HEADS + 2 * B_KV_HEADS) * B_HD
    dt = jnp.exp(jax.random.uniform(next(ks), (N_A_LAYERS, A_HEADS), f32, np.log(1e-3), np.log(1e-1)))
    return {
        "x": jax.random.normal(next(ks), (BATCH, SEQ, D), f32),
        "ffn1_norm": gain((DEPTH, D)),
        "ffn1_w_gu": nrm((DEPTH, D, 2 * D_FF), D ** -0.5),
        "ffn1_w_down": nrm((DEPTH, D_FF, D), D_FF ** -0.5),
        "mix_norm": gain((DEPTH, D)),
        "ffn2_norm": gain((DEPTH, D)),
        "ffn2_w_gu": nrm((DEPTH, D, 2 * D_FF), D ** -0.5),
        "ffn2_w_down": nrm((DEPTH, D_FF, D), D_FF ** -0.5),
        "a_w_in": nrm((N_A_LAYERS, D, a_in_cols), D ** -0.5),
        "a_w_conv": nrm((N_A_LAYERS, A_CONV, 2 * A_HEADS * A_DK + A_HEADS * A_DV), A_CONV ** -0.5),
        "a_A_log": jnp.log(jax.random.uniform(next(ks), (N_A_LAYERS, A_HEADS), f32, 1.0, 16.0)),
        "a_dt_bias": dt + jnp.log(-jnp.expm1(-dt)),
        "a_out_norm": gain((N_A_LAYERS, A_DV)),
        "a_w_out": nrm((N_A_LAYERS, A_HEADS * A_DV, D), (A_HEADS * A_DV) ** -0.5),
        "b_w_in": nrm((N_B_LAYERS, D, b_in_cols), D ** -0.5),
        "b_b_in": nrm((N_B_LAYERS, b_in_cols), 0.02),
        "b_sinks": nrm((N_B_LAYERS, B_HEADS), 1.0),
        "b_w_out": nrm((N_B_LAYERS, B_HEADS * B_HD, D), (B_HEADS * B_HD) ** -0.5),
        "b_b_out": nrm((N_B_LAYERS, D), 0.02),
        "final_norm": gain((D,)),
    }

def first_block(x, ffn1_norm, ffn1_w_gu, ffn1_w_down, mix_norm, ffn2_norm, ffn2_w_gu, ffn2_w_down,
              a_w_in, a_w_conv, a_A_log, a_dt_bias, a_out_norm, a_w_out,
              b_w_in, b_b_in, b_sinks, b_w_out, b_b_out, final_norm):
    for layer in range(DEPTH):
        x = x + 0.5 * swiglu(rmsnorm(x, ffn1_norm[layer]), ffn1_w_gu[layer], ffn1_w_down[layer])
        h = rmsnorm(x, mix_norm[layer])
        j = layer // N_MIXERS
        if layer % N_MIXERS == 0:
            y = mixer_gated_deltanet(h, a_w_in[j], a_w_conv[j], a_A_log[j], a_dt_bias[j],
                                     a_out_norm[j], a_w_out[j])
        else:
            y = mixer_sliding_window_sinks(h, b_w_in[j], b_b_in[j], b_sinks[j], b_w_out[j], b_b_out[j])
        x = x + y
        x = x + 0.5 * swiglu(rmsnorm(x, ffn2_norm[layer]), ffn2_w_gu[layer], ffn2_w_down[layer])
    return rmsnorm(x, final_norm)


DEPTH_2 = 1

HEAD_DIM = 64
ATTN_Q_HEADS = D_MODEL // (2 * HEAD_DIM)
ATTN_KV_HEADS = ATTN_Q_HEADS // 4
ATTN_GROUP = ATTN_Q_HEADS // ATTN_KV_HEADS
ATTN_WIDTH = ATTN_Q_HEADS * HEAD_DIM
KV_WIDTH = ATTN_KV_HEADS * HEAD_DIM
WINDOW = 128
BLOCK = 128
ROPE_THETA = 500000.0
ROT_DIM = HEAD_DIM // 4
RWKV_HEADS = D_MODEL // (2 * HEAD_DIM)
RWKV_WIDTH = RWKV_HEADS * HEAD_DIM
DECAY_RANK = 64
ICLR_RANK = 64
GATE_RANK = 128
N_BRANCH = 2
D_FF_2 = 4 * D_MODEL
PLE_DIM = 256
NORM_EPS = 1e-6
GN_EPS = 64e-5
O_Q = 0
O_K = O_Q + ATTN_WIDTH
O_V = O_K + KV_WIDTH
O_RWKV = O_V + KV_WIDTH
RWKV_COLS = 3 * RWKV_WIDTH + DECAY_RANK + ICLR_RANK + GATE_RANK
O_GATE = O_RWKV + RWKV_COLS
IN_COLS = O_GATE + N_BRANCH * D_MODEL


def rms_norm(x, g):
    xf = x.astype(jnp.float32)
    y = xf * lax.rsqrt(jnp.mean(xf * xf, axis=-1, keepdims=True) + NORM_EPS)
    return (y * g.astype(jnp.float32)).astype(x.dtype)

def rotary_partial(x, positions):
    half = ROT_DIM // 2
    inv_freq = jnp.power(jnp.float32(ROPE_THETA), -jnp.arange(half, dtype=jnp.float32) * 2.0 / ROT_DIM)
    ang = positions.astype(jnp.float32)[:, None] * inv_freq[None, :]
    cos = jnp.cos(ang)[None, :, None, :]
    sin = jnp.sin(ang)[None, :, None, :]
    xf = x[..., :ROT_DIM].astype(jnp.float32)
    x1, x2 = xf[..., :half], xf[..., half:]
    rot = jnp.concatenate([x1 * cos - x2 * sin, x2 * cos + x1 * sin], axis=-1).astype(x.dtype)
    return jnp.concatenate([rot, x[..., ROT_DIM:]], axis=-1)

def band_windows(t, n_blocks):
    b, _, h, d = t.shape
    tp = jnp.pad(t, ((0, 0), (BLOCK, BLOCK), (0, 0), (0, 0))).reshape(b, n_blocks + 2, BLOCK, h, d)
    return jnp.concatenate([tp[:, :-2], tp[:, 1:-1], tp[:, 2:]], axis=2)

def windowed_gqa(q, k, v, sink):
    b, s = q.shape[0], q.shape[1]
    nb = s // BLOCK
    qb = q.reshape(b, nb, BLOCK, ATTN_KV_HEADS, ATTN_GROUP, HEAD_DIM)
    kw = band_windows(k, nb)
    vw = band_windows(v, nb)
    scores = jnp.einsum('bnqhgd,bnkhd->bnhgqk', qb, kw).astype(jnp.float32) * (HEAD_DIM ** -0.5)
    qpos = jnp.arange(nb)[:, None] * BLOCK + jnp.arange(BLOCK)[None, :]
    kpos = (jnp.arange(nb)[:, None] - 1) * BLOCK + jnp.arange(3 * BLOCK)[None, :]
    valid = ((jnp.abs(qpos[:, :, None] - kpos[:, None, :]) <= WINDOW)
             & (kpos[:, None, :] >= 0) & (kpos[:, None, :] < s))
    scores = jnp.where(valid[None, :, None, None], scores, -1e30)
    sink_logit = jnp.broadcast_to(
        sink.astype(jnp.float32).reshape(ATTN_KV_HEADS, ATTN_GROUP)[None, None, :, :, None, None],
        scores.shape[:-1] + (1,))
    probs = jax.nn.softmax(jnp.concatenate([scores, sink_logit], axis=-1), axis=-1)[..., :-1]
    out = jnp.einsum('bnhgqk,bnkhd->bnqhgd', probs.astype(v.dtype), vw)
    return out.reshape(b, s, ATTN_WIDTH)

def centred_shift(z):
    prev = jnp.pad(z[:, :-1], ((0, 0), (1, 0), (0, 0)))
    nxt = jnp.pad(z[:, 1:], ((0, 0), (0, 1), (0, 0)))
    return 0.5 * (prev + nxt)

def rwkv7_bidir_scan(r, w, k, v, a, b):
    xs = (jnp.moveaxis(r, 2, 0), jnp.moveaxis(w, 2, 0), jnp.moveaxis(k, 2, 0),
          jnp.moveaxis(v, 2, 0), jnp.moveaxis(a, 2, 0), jnp.moveaxis(b, 2, 0))

    def step(state, inp):
        r_t, w_t, k_t, v_t, a_t, b_t = inp
        sa = jnp.einsum('dbhij,dbhj->dbhi', state, a_t)
        state = (state * w_t[..., None, :] + sa[..., :, None] * b_t[..., None, :]
                 + v_t[..., :, None] * k_t[..., None, :])
        y = jnp.einsum('dbhij,dbhj->dbhi', state, r_t)
        return state, y

    d, bsz, _, h, n = r.shape
    s0 = jnp.zeros((d, bsz, h, n, n), jnp.float32)
    _, ys = lax.scan(step, s0, xs)
    return jnp.moveaxis(ys, 0, 2)

def rwkv7_time_mix(z, w0, w2, a0, a2, g2, k_k, k_a, r_k, lnx_w, lnx_b):
    f32 = jnp.float32
    bsz, t = z.shape[0], z.shape[1]
    c = RWKV_WIDTH
    hn = (RWKV_HEADS, HEAD_DIM)
    r = z[..., :c]
    k = z[..., c:2 * c]
    v = z[..., 2 * c:3 * c]
    o = 3 * c
    wl = z[..., o:o + DECAY_RANK]
    o += DECAY_RANK
    al = z[..., o:o + ICLR_RANK]
    o += ICLR_RANK
    gl = z[..., o:o + GATE_RANK]
    w_raw = (w0[:, None, None, :] + jnp.einsum('btr,drc->dbtc', jnp.tanh(wl), w2)).astype(f32)
    decay = jnp.exp(-jnp.exp(-jax.nn.softplus(-w_raw) - 0.5))
    a = jax.nn.sigmoid((a0[:, None, None, :] + jnp.einsum('btr,drc->dbtc', al, a2)).astype(f32))
    g = (jax.nn.sigmoid(gl) @ g2).astype(f32)
    kk = (k * k_k).astype(f32).reshape(bsz, t, *hn)
    kk = kk / jnp.maximum(jnp.sqrt(jnp.sum(kk * kk, axis=-1, keepdims=True)), 1e-12)
    k_dir = (k.astype(f32)[None] * (1.0 + (a - 1.0) * k_a.astype(f32))).reshape(2, bsz, t, *hn)
    a_h = a.reshape(2, bsz, t, *hn)
    rh = r.astype(f32).reshape(bsz, t, *hn)
    vh = v.astype(f32).reshape(bsz, t, *hn)

    def orient(u):
        return jnp.stack([u[0], jnp.flip(u[1], axis=1)])

    def both(u):
        return jnp.stack([u, jnp.flip(u, axis=1)])

    ys = rwkv7_bidir_scan(both(rh), orient(decay.reshape(2, bsz, t, *hn)), orient(k_dir),
                          both(vh), both(-kk), orient(kk[None] * a_h))
    y = ys[0] + jnp.flip(ys[1], axis=1)
    mu = jnp.mean(y, axis=-1, keepdims=True)
    var = jnp.mean(jnp.square(y - mu), axis=-1, keepdims=True)
    y = ((y - mu) * lax.rsqrt(var + GN_EPS)).reshape(bsz, t, c) * lnx_w.astype(f32) + lnx_b.astype(f32)
    bonus = jnp.einsum('bthn,dbthn,dhn->bth', rh, k_dir, r_k.astype(f32))[..., None] * vh
    out = (y + bonus.reshape(bsz, t, c)) * g
    return out.astype(z.dtype)

def second_inputs(seed: int = 0) -> dict:
    key = jax.random.key(seed)
    ks = jax.random.split(key, 32)
    f32 = jnp.float32
    L = DEPTH_2

    def nrm(k, shape, scale):
        return jax.random.normal(k, shape, f32) * scale

    def gain(k, shape):
        return 1.0 + 0.05 * jax.random.normal(k, shape, f32)

    return {
        'x': nrm(ks[0], (BATCH, SEQ, D_MODEL), 1.0),
        'p': nrm(ks[1], (DEPTH_2, BATCH, SEQ, PLE_DIM), 1.0),
        'norm_mix': gain(ks[2], (L, D_MODEL)),
        'w_in': nrm(ks[3], (L, D_MODEL, IN_COLS), D_MODEL ** -0.5),
        'shift_mu': jax.random.uniform(ks[4], (L, RWKV_COLS), f32),
        'q_norm': gain(ks[5], (L, HEAD_DIM)),
        'k_norm': gain(ks[6], (L, HEAD_DIM)),
        'sink': nrm(ks[7], (L, ATTN_Q_HEADS), 0.5),
        'w0': jax.random.uniform(ks[8], (L, 2, RWKV_WIDTH), f32, minval=-6.0, maxval=1.0),
        'w2': nrm(ks[9], (L, 2, DECAY_RANK, RWKV_WIDTH), 0.1),
        'a0': nrm(ks[10], (L, 2, RWKV_WIDTH), 0.5),
        'a2': nrm(ks[11], (L, 2, ICLR_RANK, RWKV_WIDTH), ICLR_RANK ** -0.5),
        'g2': nrm(ks[12], (L, GATE_RANK, RWKV_WIDTH), GATE_RANK ** -0.5),
        'k_k': 0.85 + 0.05 * jax.random.normal(ks[13], (L, RWKV_WIDTH), f32),
        'k_a': gain(ks[14], (L, RWKV_WIDTH)),
        'r_k': nrm(ks[15], (L, 2, RWKV_HEADS, HEAD_DIM), 0.1),
        'lnx_w': gain(ks[16], (L, RWKV_WIDTH)),
        'lnx_b': nrm(ks[17], (L, RWKV_WIDTH), 0.02),
        'w_up_attn': nrm(ks[18], (L, ATTN_WIDTH, D_MODEL), ATTN_WIDTH ** -0.5),
        'w_up_rwkv': nrm(ks[19], (L, RWKV_WIDTH, D_MODEL), RWKV_WIDTH ** -0.5),
        'w_out': nrm(ks[20], (L, D_MODEL, D_MODEL), D_MODEL ** -0.5),
        'norm_ffn': gain(ks[21], (L, D_MODEL)),
        'w_ff1': nrm(ks[22], (L, D_MODEL, D_FF_2), D_MODEL ** -0.5),
        'w_ff2': nrm(ks[23], (L, D_FF_2, D_MODEL), D_FF_2 ** -0.5),
        'norm_ple': gain(ks[24], (L, D_MODEL)),
        'w_ple_gate': nrm(ks[25], (L, D_MODEL, D_MODEL), D_MODEL ** -0.5),
        'w_ple': nrm(ks[26], (L, PLE_DIM, D_MODEL), PLE_DIM ** -0.5),
    }

def second_block(x, p, norm_mix, w_in, shift_mu, q_norm, k_norm, sink, w0, w2, a0, a2, g2,
              k_k, k_a, r_k, lnx_w, lnx_b, w_up_attn, w_up_rwkv, w_out, norm_ffn,
              w_ff1, w_ff2, norm_ple, w_ple_gate, w_ple):
    bsz, s = x.shape[0], x.shape[1]
    positions = jnp.arange(s)
    for i in range(DEPTH_2):
        h = rms_norm(x, norm_mix[i])
        proj = h @ w_in[i]
        q = proj[..., O_Q:O_K].reshape(bsz, s, ATTN_Q_HEADS, HEAD_DIM)
        k = proj[..., O_K:O_V].reshape(bsz, s, ATTN_KV_HEADS, HEAD_DIM)
        v = proj[..., O_V:O_RWKV].reshape(bsz, s, ATTN_KV_HEADS, HEAD_DIM)
        q = rotary_partial(rms_norm(q, q_norm[i]), positions)
        k = rotary_partial(rms_norm(k, k_norm[i]), positions)
        attn = windowed_gqa(q, k, v, sink[i])
        zr = proj[..., O_RWKV:O_GATE]
        zr = zr + shift_mu[i] * (centred_shift(zr) - zr)
        rw = rwkv7_time_mix(zr, w0[i], w2[i], a0[i], a2[i], g2[i], k_k[i], k_a[i],
                            r_k[i], lnx_w[i], lnx_b[i])
        gates = jax.nn.sigmoid(proj[..., O_GATE:].reshape(bsz, s, N_BRANCH, D_MODEL))
        merged = gates[..., 0, :] * (attn @ w_up_attn[i]) + gates[..., 1, :] * (rw @ w_up_rwkv[i])
        x = x + merged @ w_out[i]
        hf = rms_norm(x, norm_ffn[i])
        x = x + jnp.square(jax.nn.relu(hf @ w_ff1[i])) @ w_ff2[i]
        hp = rms_norm(x, norm_ple[i])
        x = x + (p[i] @ w_ple[i]) * jax.nn.sigmoid(hp @ w_ple_gate[i])
    return x


def setup_inputs(seed=0):
    out = dict(first_inputs(seed))
    for name, value in second_inputs(seed + 1).items():
        if name != "x":
            out[name + "_2"] = value
    return out


def reference(
    x, ffn1_norm, ffn1_w_gu, ffn1_w_down, mix_norm, ffn2_norm, ffn2_w_gu, ffn2_w_down, a_w_in,
    a_w_conv, a_A_log, a_dt_bias, a_out_norm, a_w_out, b_w_in, b_b_in, b_sinks, b_w_out,
    b_b_out, final_norm, p_2, norm_mix_2, w_in_2, shift_mu_2, q_norm_2, k_norm_2, sink_2, w0_2,
    w2_2, a0_2, a2_2, g2_2, k_k_2, k_a_2, r_k_2, lnx_w_2, lnx_b_2, w_up_attn_2, w_up_rwkv_2,
    w_out_2, norm_ffn_2, w_ff1_2, w_ff2_2, norm_ple_2, w_ple_gate_2, w_ple_2,
):
    x = first_block(
        x, ffn1_norm, ffn1_w_gu, ffn1_w_down, mix_norm, ffn2_norm, ffn2_w_gu, ffn2_w_down,
        a_w_in, a_w_conv, a_A_log, a_dt_bias, a_out_norm, a_w_out, b_w_in, b_b_in, b_sinks,
        b_w_out, b_b_out, final_norm,
    )
    return second_block(
        x, p_2, norm_mix_2, w_in_2, shift_mu_2, q_norm_2, k_norm_2, sink_2, w0_2, w2_2, a0_2,
        a2_2, g2_2, k_k_2, k_a_2, r_k_2, lnx_w_2, lnx_b_2, w_up_attn_2, w_up_rwkv_2, w_out_2,
        norm_ffn_2, w_ff1_2, w_ff2_2, norm_ple_2, w_ple_gate_2, w_ple_2,
    )


_drawn_inputs = setup_inputs


def setup_inputs(seed=0):
    import zlib

    import numpy as np

    out = dict(_drawn_inputs(seed))
    spreads = {}
    factors = {'ffn1_norm': 3.741,
     'ffn2_norm': 4.946,
     'a_out_norm': 4.998,
     'b_sinks': 8.577,
     'q_norm_2': 8.0,
     'k_norm_2': 8.0,
     'sink_2': 8.0,
     'w2_2': 4.435,
     'k_k_2': 4.038,
     'k_a_2': 3.266,
     'lnx_w_2': 3.857,
     'lnx_b_2': 8.0,
     'norm_ple_2': 26.328,
     'b_b_in': 6.519,
     'b_b_out': 6.877}
    for name, (base, spread) in spreads.items():
        noise = np.random.default_rng([zlib.crc32(name.encode()), seed]).standard_normal(out[name].shape)
        drawn = base * np.exp(spread * noise) if base else spread * noise
        out[name] = __import__('jax').numpy.asarray(drawn.astype(out[name].dtype))
    for name, factor in factors.items():
        out[name] = (out[name] * factor).astype(out[name].dtype)
    return out
```

```python
import numpy as np
import concourse.bass as bass
from concourse import mybir

F32 = mybir.dt.float32
F32R = mybir.dt.float32r
U32 = mybir.dt.uint32
ALU = mybir.AluOpType
ACT = mybir.ActivationFunctionType
AX = mybir.AxisListType

P = 128
T = 256
NB = T // P
D = 1024
KD = D // P
D_FF = 2816
NG = D_FF // P
D_FF2 = 4096
NF = D_FF2 // P
EPS = 1e-6
GN_EPS = 64e-5
NEG = -1e30
LN_EXP = "natural_log_exp_and_others"
LEVELS = 7
PIECE = 2048
RAW_SLOTS = 4
SPLIT_SLOTS = 2
HEADS_A = 8
ZT = 14

CONST_PARTS = [
    ("ident", P), ("ones", P), ("ones_head", P), ("upto", P), ("rotate", P), ("cos", T), ("sin", T),
    ("strict_up", P), ("neg_low", P), ("band_prev", T), ("band_first", T), ("band_last", T), ("tiny", 4),
]
MASK_PARTS = [("mask_fwd", 4 * P), ("mask_bwd", 4 * P), ("merge", LEVELS * P), ("merge_t", LEVELS * P)]


def _places(parts):
    where, cols = {}, 0
    for name, n in parts:
        where[name] = (cols, cols + n)
        cols += n
    return where, cols


CONST_AT, CONST_COLS = _places(CONST_PARTS)
MASK_AT, MASK_COLS = _places(MASK_PARTS)


def constants():
    p = np.arange(P)[:, None]
    f = np.arange(P)[None, :]
    c = {}
    c["ident"] = p == f
    c["ones"] = np.ones((P, P))
    c["ones_head"] = p // 64 == f // 64
    c["upto"] = p <= f
    rot = np.zeros((P, P))
    for h in (0, 64):
        for i in range(8):
            rot[h + 8 + i, h + i] = -1.0
            rot[h + i, h + 8 + i] = 1.0
    c["rotate"] = rot
    inv = np.power(np.float32(500000.0), -np.arange(8, dtype=np.float32) * np.float32(2.0) / np.float32(16))
    ang = np.arange(T, dtype=np.float32)[None, :] * inv.astype(np.float32)[:, None]
    cos, sin = np.ones((P, T)), np.zeros((P, T))
    for h in (0, 64):
        for half in (0, 8):
            cos[h + half:h + half + 8] = np.cos(ang)
            sin[h + half:h + half + 8] = np.sin(ang)
    c["cos"], c["sin"] = cos, sin
    up, upi, lo, loi = p < f, p <= f, p > f, p >= f
    c["strict_up"] = up
    c["mask_fwd"] = np.concatenate([up, upi, up, upi], 1)
    c["mask_bwd"] = np.concatenate([up, loi, lo, loi], 1)
    c["neg_low"] = np.where(upi, 0.0, NEG)
    k = np.arange(T)[None, :]
    c["band_prev"] = np.where((k <= p + P) & (k > p), 0.0, NEG)
    c["band_first"] = np.where(k <= p + P, 0.0, NEG)
    c["band_last"] = np.where(k >= p, 0.0, NEG)
    m = []
    for lv in range(LEVELS):
        b = 1 << lv
        m.append((p // (2 * b) == f // (2 * b)) & (p // b % 2 == 1) & (f // b % 2 == 0))
    c["merge"] = np.concatenate(m, 1)
    c["merge_t"] = np.concatenate([x.T for x in m], 1)
    c["tiny"] = np.tile(np.array([[EPS, GN_EPS, 12.0 * np.log(2.0), 1.0]]), (P, 1))
    return (np.concatenate([np.asarray(c[n], np.float32) for n, _ in CONST_PARTS], 1),
            np.concatenate([np.asarray(c[n], np.float32) for n, _ in MASK_PARTS], 1))


ROWS_A = {}
ROWS_B = {}


def _rows():
    at = 0
    for name, n in (("ffn1_norm", 16), ("mix_norm", 16), ("ffn2_norm", 16), ("norm_mix_2", 8),
                    ("norm_ffn_2", 8), ("norm_ple_2", 8), ("b_b_in", 12), ("b_b_out", 8), ("shift_mu_2", 14),
                    ("final_norm", 8), ("k_a_2", 4), ("lnx_w_2", 4), ("lnx_b_2", 4)):
        ROWS_A[name] = (at, n)
        at += n
    n_a = at
    at = 0
    for name, n in (("a_w_conv", 96), ("w0_2", 8), ("a0_2", 8), ("r_k_2", 8), ("a_out_norm", 1),
                    ("q_norm_2", 1), ("k_norm_2", 1), ("k_k_2", 4)):
        ROWS_B[name] = (at, n)
        at += n
    return n_a, at


N_ROWS_A, N_ROWS_B = _rows()

JOBS = [("gu0", "narrow", 11), ("down0", "wide", 11), ("a_in", "narrow", 8), ("a_out", "wide", 4),
        ("gu1", "narrow", 11), ("down1", "wide", 11), ("gu2", "narrow", 11), ("down2", "wide", 11),
        ("b_in", "narrow", 3), ("b_out", "wide", 4), ("gu3", "narrow", 11), ("down3", "wide", 11),
        ("in2", "narrow", 9), ("up_attn", "wide", 2), ("up_rwkv", "wide", 2), ("out2", "wide", 4),
        ("ff1", "narrow", 8), ("ff2", "wide", 16), ("ple", "wide", 1), ("ple_gate", "wide", 4)]
PIECE_OF, FILL_OF, COUNT_OF = {}, {}, {}
_p = _f = 0
for _name, _kind, _n in JOBS:
    PIECE_OF[_name], FILL_OF[_name], COUNT_OF[_name] = _p, _f, _n
    _p += 2 * _n if _kind == "narrow" else _n
    _f += _n if _kind == "narrow" else 2
PIECES = _p
IN_DMAS = 36


class Map:

    def __init__(self, nc, at, end):
        self.nc, self.at, self.end = nc, at, end

    def take(self, name, shape, dt=F32):
        n = 1
        for x in shape[1:]:
            n *= x
        n *= 1 if dt == mybir.dt.uint8 else 4
        t = self.nc.alloc_sbuf_tensor_at(name, list(shape), dt, offset=self.at)
        self.at += -(-n // 32) * 32
        assert self.at <= self.end, (name, self.at, self.end)
        return t


class Chain:

    def __init__(self, eng, sem):
        self.eng, self.sem, self.n, self.turn = eng, sem, 0, 0

    def __call__(self, ins):
        self.n += 1
        ins.then_inc(self.sem, 1)
        self.eng.wait_ge(self.sem, self.n + self.turn)


def repeat(eng, n, body, chain=None, links=0):
    if n == 0:
        return
    if n == 1:
        body(0)
        return
    start = chain.n if chain else 0
    with eng.Fori(0, n) as i:
        if chain:
            chain.turn = i * links
        body(i)
    if chain:
        assert chain.n - start == links, (chain.n - start, links)
        chain.turn, chain.n = 0, start + links * n


def build(nc, A, out, stop=None):
    base = -(-16481 // 32) * 32
    fixed = Map(nc, base, 229344)
    raw = fixed.take("raw", [P, RAW_SLOTS, PIECE])
    w_hi = fixed.take("w_hi", [P, SPLIT_SLOTS, PIECE], F32R)
    w_lo = fixed.take("w_lo", [P, SPLIT_SLOTS, PIECE], F32R)
    xT = fixed.take("xT", [P, KD, T])
    cst = fixed.take("cst", [P, CONST_COLS])
    msk = fixed.take("msk", [P, MASK_COLS], mybir.dt.uint8)
    cols = fixed.take("cols", [P, 2 * P])
    bcast = fixed.take("bcast", [P, 40])
    p_hi = fixed.take("p_hi", [P, 2, T], F32R)
    p_lo = fixed.take("p_lo", [P, 2, T], F32R)
    ba_raw = fixed.take("ba_raw", [P, KD, 16])
    small = fixed.take("small", [P, 64])
    scratch_at = fixed.at
    sq = fixed.take("sq", [P, KD, T])
    rstd = fixed.take("rstd", [P, T])
    full3 = fixed.take("full3", [P, 3, 2, T])
    h_at = fixed.at
    h_hi = fixed.take("h_hi", [P, KD, T], F32R)
    h_lo = fixed.take("h_lo", [P, KD, T], F32R)
    arena = fixed.at
    end = 229344

    m = Map(nc, arena, end)
    g_hi = m.take("g_hi", [P, NF, T], F32R)
    g_lo = m.take("g_lo", [P, NF, T], F32R)
    act2 = m.take("act2", [P, 2, 2, T])
    full2 = m.take("full2", [P, 2, 2, T])
    m = Map(nc, arena, end)
    rows = m.take("rows", [P, 2, P])
    x_tok = m.take("x_tok", [P, NB, D])
    p_tok = m.take("p_tok", [P, NB, 2 * P])
    mask_f32 = m.take("mask_f32", [P, MASK_COLS])
    m = Map(nc, arena, end)
    y_tok = m.take("y_tok", [P, NB, D])
    def constant(name):
        a, b = CONST_AT[name]
        return cst[:, a:b]

    def mask8(name):
        a, b = MASK_AT[name]
        return msk[:, a:b]

    def column(name, i=0):
        if name in ROWS_A:
            return cols[:, ROWS_A[name][0] + i:ROWS_A[name][0] + i + 1]
        return cols[:, P + ROWS_B[name][0] + i:P + ROWS_B[name][0] + i + 1]

    ident = constant("ident")
    ones = constant("ones")
    ones_head = constant("ones_head")
    eps_col = cst[:, CONST_AT["tiny"][0]:CONST_AT["tiny"][0] + 1]

    one_col = cst[:, CONST_AT["tiny"][0] + 3:CONST_AT["tiny"][0] + 4]

    D_ps = nc.alloc_psum_tensor("dense_ps", [P, 4, 512], F32)
    M_ps = nc.alloc_psum_tensor("mixer_ps", [P, 4, 512], F32)

    sems = {}

    def sem(name):
        if name not in sems:
            sems[name] = nc.alloc_semaphore(name)
        return sems[name]

    def alone(eng):
        eng.nop().then_inc(sem("passed"), 1)

    raw_loaded = [sem(f"raw_loaded{i}") for i in range(RAW_SLOTS)]
    hi_ready = sem("hi_ready")
    lo_ready = sem("lo_ready")
    piece_used = sem("piece_used")
    half_filled = sem("half_filled")
    dense_drained = sem("dense_drained")
    sq_ready = sem("sq_ready")
    sq_folded = sem("sq_folded")
    sq_summed = sem("sq_summed")
    gate_scaled = sem("gate_scaled")
    ss_ready = sem("ss_ready")
    rstd_ready = sem("rstd_ready")
    h_ready = sem("h_ready")
    act_ready = sem("act_ready")
    g_ready = sem("g_ready")
    const_loaded, in_loaded = sem("const_loaded"), sem("in_loaded")
    start_turned = sem("start_turned")
    mask_loaded, mask_kept = sem("mask_loaded"), sem("mask_kept")
    out_turned, out_kept, out_stored = sem("out_turned"), sem("out_kept"), sem("out_stored")

    gated = {"gu0": ("ffn1_w_gu", 0), "gu1": ("ffn2_w_gu", 0), "gu2": ("ffn1_w_gu", 1), "gu3": ("ffn2_w_gu", 1)}
    downs = {"down0": ("ffn1_w_down", 0), "down1": ("ffn2_w_down", 0), "down2": ("ffn1_w_down", 1),
             "down3": ("ffn2_w_down", 1)}
    others = {"a_in": "a_w_in", "a_out": "a_w_out", "b_in": "b_w_in", "b_out": "b_w_out", "in2": "w_in_2",
              "up_attn": "w_up_attn_2", "up_rwkv": "w_up_rwkv_2", "out2": "w_out_2", "ff1": "w_ff1_2",
              "ff2": "w_ff2_2", "ple": "w_ple_2", "ple_gate": "w_ple_gate_2"}

    STAGES = ["start", "ffn0", "mixer_a", "ffn1", "ffn2", "mixer_b", "ffn3", "final_norm", "hybrid",
              "ffn4", "ple", "finish"]
    if stop:
        STAGES = STAGES[:STAGES.index(stop) + 1] + ["finish"]
    jobs_of = {"ffn0": ["gu0", "down0"], "mixer_a": ["a_in", "a_out"], "ffn1": ["gu1", "down1"],
               "ffn2": ["gu2", "down2"], "mixer_b": ["b_in", "b_out"], "ffn3": ["gu3", "down3"],
               "hybrid": ["in2", "up_attn", "up_rwkv", "out2"], "ffn4": ["ff1", "ff2"],
               "ple": ["ple", "ple_gate"]}
    jobs = [j for s in STAGES for j in jobs_of.get(s, [])]
    kind_of = {n: k for n, k, _ in JOBS}
    pieces_of = {n: 2 * c if k == "narrow" else c for n, k, c in JOBS}
    n_pieces = PIECE_OF[jobs[-1]] + pieces_of[jobs[-1]] if jobs else 0
    NORM = {"ffn0": 0, "mixer_a": 1, "ffn1": 2, "ffn2": 3, "mixer_b": 4, "ffn3": 5, "final_norm": 6,
            "hybrid": 7, "ffn4": 8, "ple": 9}
    NORM_COL = {"ffn0": ("ffn1_norm", 0), "mixer_a": ("mix_norm", 0), "ffn1": ("ffn2_norm", 0),
                "ffn2": ("ffn1_norm", 8), "mixer_b": ("mix_norm", 8), "ffn3": ("ffn2_norm", 8),
                "final_norm": ("final_norm", 0), "hybrid": ("norm_mix_2", 0), "ffn4": ("norm_ffn_2", 0),
                "ple": ("norm_ple_2", 0)}

    BEFORE = {"mixer_a": "down0", "ffn1": "a_out", "ffn2": "down1", "mixer_b": "down2", "ffn3": "b_out",
              "final_norm": "down3", "ffn4": "out2", "ple": "ff2"}
    chunk_of = {}
    n_chunks = 0
    for j in ("gu0", "gu1", "gu2", "gu3", "ff1"):
        chunk_of[j] = n_chunks
        n_chunks += COUNT_OF[j]

    LATE_SCALE = [s for s in STAGES if s in ("ffn0", "ffn1", "ffn2", "ffn3", "ffn4")]
    stage_of = {j: s for s, js in jobs_of.items() for j in js}
    wide_jobs = [n for n, k, _ in JOBS if k == "wide"]
    x_ready = sem("x_ready")
    x_final = sem("x_final")

    def x_ready_at(stage):
        return 1 if stage == "ffn0" else 2

    def fill_before(stage):
        return FILL_OF[BEFORE[stage]] if stage in BEFORE else None

    def h_before(stage):
        return 4 * (NORM[stage] - (NORM[stage] > NORM["final_norm"]))

    def wait_half(eng, job, e):
        if e == 0:
            eng.wait_ge(half_filled, wide_jobs.index(job) + 1)
        else:
            eng.wait_ge(piece_used, PIECE_OF[job] + pieces_of[job])

    HEAD_PIECES = [PIECE_OF["b_in"] + i for i in range(4)] + [PIECE_OF["in2"] + i for i in range(2)]

    def by_heads(tensor, slot, k):
        return tensor[:, slot, 512 * k:512 * k + 512].rearrange("p (s t d) -> p t s d", s=2, t=4)

    def as_heads(tensor, slot, k):
        return tensor[:, slot, 512 * k:512 * k + 512].rearrange("p (t s d) -> p t s d", s=2, t=4)

    GROUPS_A = 2
    NEED_A = ((0, 0), (0, 4))
    HG = HEADS_A // GROUPS_A
    m = Map(nc, arena, end)
    qkv = m.take("qkv", [P, 24, T])
    z_gate = m.take("z_gate", [P, 8, T])
    gates = m.take("gates_a", [P, 12, 16])
    per_group = m.at
    ba_hi = m.take("ba_hi", [P, KD, P], F32R)
    ba_lo = m.take("ba_lo", [P, KD, P], F32R)
    ba_fm = m.take("ba_fm", [16, T])
    m.at = per_group
    o_hi = m.take("o_hi", [P, 8, T], F32R)
    o_lo = m.take("o_lo", [P, 8, T], F32R)
    m.at = per_group
    qn = m.take("qn", [P, HG, T])
    kn = m.take("kn", [P, HG, T])
    k_tok = m.take("k_tok", [P, 8, P])
    v_tok = m.take("v_tok", [P, 8, P])
    dec_t = m.take("dec_t", [P, 8, P])
    neg_lt = m.take("neg_lt", [P, 8, P])
    att_t = m.take("att_t", [P, 8, P])
    v_new = m.take("v_new", [P, 2, HG, P])
    q_dec = m.take("q_dec", [P, HG, P])
    k_dec = m.take("k_dec", [P, HG, P])
    state = m.take("state_a", [P, HG, P])
    at = m.at
    inv = m.take("inv_a", [P, 8, P])
    m.at = at
    g_upto = m.take("g_upto", [P, 8, P])
    at = m.at
    inv_t = m.take("inv_t_a", [P, 8, P])
    m.at = at
    v_now = m.take("v_now", [P, HG, T])
    at = m.at
    ly = m.take("ly_a", [P, 8, P])
    m.at = at
    dec_strict = m.take("dec_strict", [P, 8, P])
    m.at = at
    rest = m.take("rest_a", [P, HG, P])
    m.at = at + 8 * P * 4
    e_row = m.take("e_row", [P, HG, P])
    A_END = m.at
    (X_A, X_POS, X_ABS, E_ABS, SOFT, E_B, G_LOG, BETA, NBETA, G_CUM, NEG_EG, K_DECAY) = range(12)

    def gate(i):
        return gates[:, i, :].rearrange("p (h b) -> p h b", b=2)

    def over_free(ap, n):
        return ap.unsqueeze(2).to_broadcast((P, ap.shape[1], n))

    def over_mid(ap, n):
        return ap.unsqueeze(1).to_broadcast((P, n, ap.shape[1]))

    def banks(first, n, tensor=None):
        t = M_ps if tensor is None else tensor
        return t[:, first:first + n, :].rearrange("p b (s i) -> p (b s) i", i=P)

    a_taps, a_conv, a_z = sem("a_taps"), sem("a_conv"), sem("a_z")
    ba_ready, ba_done, ba_kept, ba_turned = sem("ba_ready"), sem("ba_done"), sem("ba_kept"), sem("ba_turned")
    a_gate = [sem(f"a_gate{i}") for i in range(7)]
    a_free, a_sq, a_ss, a_rs, a_qk, a_vnow = (sem(f"a_{n}") for n in ("free", "sq", "ss", "rs", "qk", "vnow"))
    a_turned, a_ktok, a_vtok, a_gupto, a_grow = (sem(f"a_{n}") for n in ("turned", "ktok", "vtok", "gupto", "grow"))
    a_dsub, a_dexp, a_strict, a_gram, a_lt, a_init = (
        sem(f"a_{n}") for n in ("dsub", "dexp", "strict", "gram", "lt", "init"))
    a_kdec, a_v0, a_vn0, a_s, a_state, a_ks, a_rest, a_v1, a_vn1, a_o, a_osq, a_oss, a_ors, a_osplit = (
        sem(f"a_{n}") for n in ("kdec", "v0", "vn0", "s", "state", "ks", "rest", "v1", "vn1", "o", "osq", "oss",
                                "ors", "osplit"))
    y_mm, y_kept, z_mm, inv_up = sem("y_mm"), sem("y_kept"), sem("z_mm"), sem("inv_up")

    def inverse_pe(pe, nt_of, x, xt, y, ready, batch, last):
        for lv in range(LEVELS):
            for half in range(2):
                if lv == 0:
                    if half == 0:
                        for s_, n_ in ready:
                            pe.wait_ge(s_, n_)
                else:
                    pe.wait_ge(inv_up, 14 * batch + 2 * (lv - 1) + half + 1)
                for s_ in range(4 * half, 4 * half + 4):
                    end_ = pe.matmul(M_ps[:, half, P * (s_ % 4):P * (s_ % 4) + P], nt_of(s_), x[:, s_, :],
                                     start=True, stop=True)
                end_.then_inc(y_mm, 1)
            if lv == 0:
                continue
            for half in range(2):
                pe.wait_ge(y_kept, 12 * batch + 2 * (lv - 1) + half + 1)
                for s_ in range(4 * half, 4 * half + 4):
                    o_ = slice(P * (s_ % 4), P * (s_ % 4) + P)
                    if lv < LEVELS - 1 or s_ % 4 in range(*last[0]):
                        end_ = pe.matmul(M_ps[:, 2 + half, o_], xt[:, s_, :], y[:, s_, :], start=True, stop=True)
                    if lv < LEVELS - 1 or s_ % 4 in range(*last[1]):
                        end_ = pe.matmul(D_ps[:, half, o_], y[:, s_, :], xt[:, s_, :], start=True, stop=True)
                end_.then_inc(z_mm, 1)

    def inverse_act(act, y, batch):
        for lv in range(1, LEVELS):
            for half in range(2):
                act.wait_ge(y_mm, 14 * batch + 2 * lv + half + 1)
                act.activation(y[:, 4 * half:4 * half + 4, :], banks(half, 1), ACT.Copy).then_inc(y_kept, 1)

    def inverse_dve(dve, nt4_of, x, xt, batch, last):
        for lv in range(LEVELS):
            for half in range(2):
                if lv == 0:
                    dve.wait_ge(y_mm, 14 * batch + half + 1)
                else:
                    dve.wait_ge(z_mm, 12 * batch + 2 * (lv - 1) + half + 1)
                alone(dve)
                for i, (out_, name) in enumerate(((x, "merge"), (xt, "merge_t"))):
                    a, b = last[i] if lv == LEVELS - 1 else (0, 4)
                    if a == b:
                        continue
                    if lv == 0:
                        data = nt4_of(half) if i else banks(half, 1)
                    else:
                        data = (banks(half, 1, D_ps) if i else banks(2 + half, 1))[:, a:b, :]
                    end_ = dve.copy_predicated(out=out_[:, 4 * half + a:4 * half + b, :],
                                               mask=over_mid(mask8(name)[:, P * lv:P * lv + P], b - a), data=data)
                end_.then_inc(inv_up, 1)

    def mixer_a_pe(pe, run_narrow, wide):
        run_narrow("a_in")
        pe.wait_ge(ba_ready, 1)
        for k in range(KD):
            pe.matmul(M_ps[:, 0, 0:T], ba_hi[:, k, :], h_hi[:, k, :], start=k == 0, stop=False)
            pe.matmul(M_ps[:, 0, 0:T], ba_hi[:, k, :], h_lo[:, k, :], start=False, stop=False)
            last = pe.matmul(M_ps[:, 0, 0:T], ba_lo[:, k, :], h_hi[:, k, :], start=False, stop=k == KD - 1)
        last.then_inc(ba_done, 1)
        pe.wait_ge(ba_kept, 1)
        for b in range(NB):
            last = pe.transpose(M_ps[:, 1, 16 * b:16 * b + 16], ba_fm[:, P * b:P * b + P], ident[0:16, 0:16])
        last.then_inc(ba_turned, 1)
        pe.wait_ge(a_gate[2], 1)
        pe.matmul(M_ps[:, 2, 0:16], constant("upto"), gates[:, G_LOG, :], start=True, stop=True)
        pe.matmul(M_ps[:, 2, 16:32], ones, gates[:, G_LOG, :], start=True, stop=True).then_inc(a_gate[3], 1)
        pe.wait_ge(dense_drained, 2 + FILL_OF["a_in"] + COUNT_OF["a_in"])

        def group(g):
            pe.wait_ge(a_free, g + 1)
            pe.wait_ge(a_sq, g + 1)
            for k in range(4):
                last = pe.matmul(M_ps[:, k, :], ones, sq[:, 2 * k:2 * k + 2, :].rearrange("p a t -> p (a t)"),
                                 start=True, stop=True)
            last.then_inc(a_ss, 1)
            pe.wait_ge(a_qk, g + 1)
            pe.wait_ge(a_vnow, g + 1)
            for h in range(HG):
                for b in range(NB):
                    pe.transpose(banks(0, 2)[:, 2 * h + b, :], kn[:, h, P * b:P * b + P], ident)
                    last = pe.transpose(banks(2, 2)[:, 2 * h + b, :], v_now[:, h, P * b:P * b + P], ident)
            last.then_inc(a_turned, 1)
            pe.wait_ge(a_ktok, g + 1)
            pe.wait_ge(a_gupto, g + 1)
            for k in range(2):
                last = pe.matmul(M_ps[:, k, :], ones, g_upto[:, 4 * k:4 * k + 4, :].rearrange("p s i -> p (s i)"),
                                 start=True, stop=True)
            last.then_inc(a_grow, 1)
            pe.wait_ge(a_vtok, g + 1)
            for h in range(HG):
                for b in range(NB):
                    kb = kn[:, h, P * b:P * b + P]
                    pe.matmul(banks(2, 2)[:, 2 * h + b, :], kb, kb, start=True, stop=True)
                    last = pe.matmul(banks(0, 2, D_ps)[:, 2 * h + b, :], kb, qn[:, h, P * b:P * b + P],
                                     start=True, stop=True)
            last.then_inc(a_gram, 1)
            inverse_pe(pe, lambda s_: neg_lt[:, s_, :], inv, inv_t, ly,
                       [(a_lt, g + 1), (a_init, g + 1)], g, NEED_A)
            for half in range(2):
                pe.wait_ge(inv_up, 14 * g + 13 + half)
            for h in range(HG):
                last = pe.matmul(banks(0, 1)[:, h, :], inv_t[:, 2 * h, :], v_tok[:, 2 * h, :], start=True, stop=True)
            last.then_inc(a_v0, 1)
            pe.wait_ge(a_vn0, g + 1)
            pe.wait_ge(a_kdec, g + 1)
            for h in range(HG):
                last = pe.matmul(banks(1, 1)[:, h, :], k_dec[:, h, :], v_new[:, 0, h, :], start=True, stop=True)
            last.then_inc(a_s, 1)
            pe.wait_ge(a_state, g + 1)
            for h in range(HG):
                last = pe.matmul(banks(0, 1)[:, h, :], kn[:, h, P:T], state[:, h, :], start=True, stop=True)
            last.then_inc(a_ks, 1)
            pe.wait_ge(a_rest, g + 1)
            for h in range(HG):
                last = pe.matmul(banks(1, 1)[:, h, :], inv_t[:, 2 * h + 1, :], rest[:, h, :], start=True, stop=True)
            last.then_inc(a_v1, 1)
            pe.wait_ge(a_vn1, g + 1)
            for h in range(HG):
                pe.matmul(banks(2, 2)[:, 2 * h, :], v_new[:, 0, h, :], att_t[:, 2 * h, :], start=True, stop=True)
                pe.matmul(banks(2, 2)[:, 2 * h + 1, :], v_new[:, 1, h, :], att_t[:, 2 * h + 1, :],
                          start=True, stop=False)
                last = pe.matmul(banks(2, 2)[:, 2 * h + 1, :], state[:, h, :], q_dec[:, h, :],
                                 start=False, stop=True)
            last.then_inc(a_o, 1)
            pe.wait_ge(a_osq, g + 1)
            for k in range(2):
                last = pe.matmul(M_ps[:, k, :], ones, sq[:, 2 * k:2 * k + 2, :].rearrange("p a t -> p (a t)"),
                                 start=True, stop=True)
            last.then_inc(a_oss, 1)
        repeat(pe, GROUPS_A, group)
        wide("a_out", o_hi, o_lo, (a_osplit, 0))

    def mixer_a_act(act, link, narrow, splits):
        f0 = FILL_OF["a_in"]

        def conv(c, q):
            alone(act)
            if q:
                act.wait_ge(a_conv, c)
                alone(act)
                act.activation(qkv[:, bass.ds(4 * c - 4, 4), :], qkv[:, bass.ds(4 * c - 4, 4), :], ACT.Silu)
            for i in range(4):
                ps = D_ps[:, 2 * ((f0 + q) % 2) + i // 2, T * (i % 2):T * (i % 2) + T]
                w = cols[:, bass.ds(P + ROWS_B["a_w_conv"][0] + 72 + i + 4 * c, 1)]
                last = act.activation(qkv[:, bass.ds(4 * c + i, 1), :].rearrange("p a t -> p (a t)"), ps,
                                      ACT.Copy, scale=w)
            last.then_inc(a_taps, 1)
            if q:
                act.wait_ge(a_conv, c + 1)
                alone(act)
                link(act.activation(qkv[:, bass.ds(4 * c, 4), :], qkv[:, bass.ds(4 * c, 4), :], ACT.Silu))
        act.preload_act_table(ACT.Silu)
        narrow("a_in", conv, 1, 0, 6)

        def z(c, q):
            act.activation(z_gate[:, 4 * c:4 * c + 4, :], D_ps[:, 2 * ((f0 + q) % 2):2 * ((f0 + q) % 2) + 2, :]
                           .rearrange("p a (k t) -> p (a k) t", t=T), ACT.Silu).then_inc(a_z, 1)
        narrow("a_in", z, 0, 6, 2)
        act.preload_act_table_set(LN_EXP)
        act.wait_ge(ba_done, 1)
        act.activation(ba_fm[:, :], M_ps[0:16, 0, 0:T], ACT.Copy).then_inc(ba_kept, 1)
        act.wait_ge(a_gate[0], 1)
        act.activation(gates[:, E_ABS, :], gates[:, X_ABS, :], ACT.Exp, scale=-1.0)
        act.activation(gate(E_B), M_ps[:, 1, 0:32].rearrange("p (b n) -> p n b", b=2)[:, 0:8, :], ACT.Exp,
                       scale=-1.0)
        link(act.activation(small[:, 0:8], bcast[:, 0:8], ACT.Exp))
        act.activation(gates[:, SOFT, :], gates[:, E_ABS, :], ACT.Ln, bias=one_col).then_inc(a_gate[1], 1)
        act.wait_ge(a_gate[3], 1)
        act.activation(gates[:, G_CUM, :], M_ps[:, 2, 0:16], ACT.Copy)
        act.activation(gates[:, NEG_EG, :], M_ps[:, 2, 0:16], ACT.Exp).then_inc(a_gate[4], 1)
        act.wait_ge(a_gate[5], 1)
        act.activation(gates[:, K_DECAY, :], gates[:, K_DECAY, :], ACT.Exp).then_inc(a_gate[6], 1)

        def group(g):
            act.wait_ge(a_free, g + 1)
            alone(act)
            act.activation(sq[:, 0:4, :], qkv[:, bass.ds(4 * g, 4), :], ACT.Square)
            act.activation(sq[:, 4:8, :], qkv[:, bass.ds(4 * g + 8, 4), :], ACT.Square).then_inc(a_sq, 1)
            act.activation(v_now[:, :, :], qkv[:, bass.ds(4 * g + 16, 4), :], ACT.Copy).then_inc(a_vnow, 1)
            act.wait_ge(a_ss, g + 1)
            sq2 = sq[:, :, :].rearrange("p a t -> p (a t)")
            link(act.activation(sq2, M_ps[:, :, :].rearrange("p a t -> p (a t)"), ACT.Ln, bias=eps_col))
            act.activation(sq2, sq2, ACT.Exp, scale=-0.5).then_inc(a_rs, 1)
            act.wait_ge(a_turned, g + 1)
            act.activation(k_tok[:, :, :], banks(0, 2), ACT.Copy).then_inc(a_ktok, 1)
            act.wait_ge(a_dsub, g + 1)
            act.activation(e_row[:, :, :], banks(0, 2).rearrange("p (h b) i -> p b h i", b=2)[:, 1], ACT.Exp)
            act.activation(dec_t[:, :, :], dec_t[:, :, :], ACT.Exp).then_inc(a_dexp, 1)
            inverse_act(act, ly, g)
            act.wait_ge(a_s, g + 1)
            act.activation(state[:, :, :], banks(1, 1), ACT.Copy).then_inc(a_state, 1)
            act.wait_ge(a_o, g + 1)
            act.activation(sq[:, 0:4, :].rearrange("p a t -> p (a t)"),
                           M_ps[:, 2:4, :].rearrange("p a t -> p (a t)"), ACT.Square).then_inc(a_osq, 1)
            act.wait_ge(a_oss, g + 1)
            r2 = sq[:, 4:8, :].rearrange("p a t -> p (a t)")
            link(act.activation(r2, M_ps[:, 0:2, :].rearrange("p a t -> p (a t)"), ACT.Ln, bias=eps_col,
                                scale=1.0 / P))
            act.activation(r2, r2, ACT.Exp, scale=-0.5).then_inc(a_ors, 1)
        repeat(act, GROUPS_A, group, link, 2)
        splits(3)

    def mixer_a_pool(pool):
        def group(g):
            pool.wait_ge(a_grow, g + 1)
            alone(pool)
            pool.tensor_copy(inv[:, :, :], over_mid(ident, 8))
            pool.tensor_copy(inv_t[:, :, :], over_mid(ident, 8)).then_inc(a_init, 1)
            pool.wait_ge(a_ktok, g + 1)
            if not isinstance(g, int) or g == 0:
                pool.wait_ge(a_gate[6], 1)
            pool.tensor_tensor(k_dec[:, :, :], k_tok[:, :, :].rearrange("p (h b) i -> p b h i", b=2)[:, 0],
                               over_free(gate(K_DECAY)[:, bass.ds(4 * g, 4), 0], P), ALU.mult).then_inc(a_kdec, 1)
            pool.wait_ge(a_dexp, g + 1)
            pool.tensor_tensor(dec_strict[:, :, :], dec_t[:, :, :], over_mid(constant("strict_up"), 8),
                               ALU.mult).then_inc(a_strict, 1)
        repeat(pool, GROUPS_A, group)

    def mixer_a_dve(dve, link, narrow, splits, split_act):
        f0 = FILL_OF["a_in"]
        dve.memset(ba_hi[:, :, :].bitcast(F32), 0.0)
        link(dve.memset(ba_lo[:, :, :].bitcast(F32), 0.0))
        split_act(ba_raw[:, :, :], ba_hi[:, :, 0:16], ba_lo[:, :, 0:16]).then_inc(ba_ready, 1)

        def conv(c, q):
            dve.wait_ge(a_taps, c + 1)
            for tap in (1, 2, 3):
                for i in range(4):
                    ps = D_ps[:, 2 * ((f0 + q) % 2) + i // 2, T * (i % 2):T * (i % 2) + T - tap]
                    w = cols[:, bass.ds(P + ROWS_B["a_w_conv"][0] + 24 * (3 - tap) + i + 4 * c, 1)]
                    o_ = qkv[:, bass.ds(4 * c + i, 1), tap:T].rearrange("p a t -> p (a t)")
                    last = dve.scalar_tensor_tensor(out=o_, in0=ps, scalar=w, in1=o_, op0=ALU.mult, op1=ALU.add)
                if tap < 3:
                    link(last)
            last.then_inc(dense_drained, 1)
            dve.wait_ge(dense_drained, 2 + f0 + c + 1)
            dve.nop().then_inc(a_conv, 1)
        narrow("a_in", conv, 2, 0, 6)

        def z(c, q):
            dve.wait_ge(a_z, c + 1)
            zc = z_gate[:, 4 * c:4 * c + 4, :]
            dve.tensor_scalar(zc, zc, column("a_out_norm"), None, ALU.mult).then_inc(dense_drained, 1)
        narrow("a_in", z, 0, 6, 2)
        dve.wait_ge(ba_turned, 1)
        a_log = M_ps[:, 1, 0:32].rearrange("p (b n) -> p n b", b=2)[:, 8:16, :]
        link(dve.tensor_tensor(gate(X_A), a_log, over_free(bcast[:, 8:16], 2), ALU.add))
        link(dve.tensor_scalar(gates[:, X_POS, :], gates[:, X_A, :], 0.0, None, ALU.max))
        dve.scalar_tensor_tensor(out=gates[:, X_ABS, :], in0=gates[:, X_POS, :], scalar=2.0,
                                 in1=gates[:, X_A, :], op0=ALU.mult, op1=ALU.subtract).then_inc(a_gate[0], 1)
        dve.wait_ge(a_gate[1], 1)
        link(dve.tensor_tensor(gates[:, SOFT, :], gates[:, SOFT, :], gates[:, X_POS, :], ALU.add))
        dve.scalar_tensor_tensor(out=gate(G_LOG), in0=gate(SOFT), scalar=-1.0, in1=over_free(small[:, 0:8], 2),
                                 op0=ALU.mult, op1=ALU.mult).then_inc(a_gate[2], 1)
        link(dve.tensor_scalar(gates[:, E_B, :], gates[:, E_B, :], 1.0, None, ALU.add))
        link(dve.reciprocal(gates[:, BETA, :], gates[:, E_B, :]))
        dve.tensor_scalar(gates[:, NBETA, :], gates[:, BETA, :], -1.0, None, ALU.mult)
        dve.wait_ge(a_gate[4], 1)
        dve.tensor_scalar(gates[:, NEG_EG, :], gates[:, NEG_EG, :], -1.0, None, ALU.mult)
        link(dve.tensor_tensor(gates[:, K_DECAY, :], M_ps[:, 2, 16:32], gates[:, G_CUM, :], ALU.subtract))
        dve.nop().then_inc(a_gate[5], 1)
        dve.nop().then_inc(a_free, 1)

        def group(g):
            g4 = bass.ds(4 * g, 4)
            dve.wait_ge(a_rs, g + 1)
            q_rs, k_rs = sq[:, 0:4, :], sq[:, 4:8, :]
            dve.scalar_tensor_tensor(out=qn[:, :, :], in0=qkv[:, g4, :], scalar=float(P) ** -0.5, in1=q_rs,
                                     op0=ALU.mult, op1=ALU.mult)
            dve.tensor_tensor(kn[:, :, :], qkv[:, bass.ds(4 * g + 8, 4), :], k_rs, ALU.mult).then_inc(a_qk, 1)
            g_now = gate(G_LOG)[:, g4, :].rearrange("p h b -> p (h b)")
            dve.tensor_tensor(g_upto[:, :, :], over_mid(constant("upto"), 8), over_free(g_now, P),
                              ALU.mult).then_inc(a_gupto, 1)
            dve.wait_ge(a_turned, g + 1)
            dve.tensor_copy(v_tok[:, :, :], banks(2, 2)).then_inc(a_vtok, 1)
            dve.wait_ge(a_grow, g + 1)

            def col(i, s_):
                return gates[:, i, bass.ds(8 * g + s_, 1)]
            for s_ in range(8):
                last = dve.scalar_tensor_tensor(out=dec_t[:, s_, :], in0=banks(0, 2)[:, s_, :], scalar=col(G_CUM, s_),
                                                in1=constant("neg_low"), op0=ALU.subtract, op1=ALU.add)
            last.then_inc(a_dsub, 1)
            dve.wait_ge(a_dexp, g + 1)
            dve.tensor_tensor(q_dec[:, :, :], qn[:, :, P:T], e_row[:, :, :], ALU.mult)
            dve.wait_ge(a_gram, g + 1)
            dve.tensor_tensor(att_t[:, :, :], banks(0, 2, D_ps), dec_t[:, :, :], ALU.mult)
            dve.wait_ge(a_strict, g + 1)
            for s_ in range(8):
                last = dve.scalar_tensor_tensor(out=neg_lt[:, s_, :], in0=banks(2, 2)[:, s_, :],
                                                scalar=col(NBETA, s_), in1=dec_strict[:, s_, :],
                                                op0=ALU.mult, op1=ALU.mult)
            last.then_inc(a_lt, 1)
            inverse_dve(dve, lambda half: neg_lt[:, 4 * half:4 * half + 4, :], inv, inv_t, g, NEED_A)
            dve.wait_ge(a_v0, g + 1)
            dve.tensor_tensor(v_new[:, 0, :, :], banks(0, 1), over_free(gate(BETA)[:, g4, 0], P),
                              ALU.mult).then_inc(a_vn0, 1)
            dve.wait_ge(a_ks, g + 1)
            for h in range(HG):
                last = dve.scalar_tensor_tensor(out=rest[:, h, :], in0=banks(0, 1)[:, h, :],
                                                scalar=col(NEG_EG, 2 * h + 1), in1=v_tok[:, 2 * h + 1, :],
                                                op0=ALU.mult, op1=ALU.add)
            last.then_inc(a_rest, 1)
            dve.wait_ge(a_v1, g + 1)
            dve.tensor_tensor(v_new[:, 1, :, :], banks(1, 1), over_free(gate(BETA)[:, g4, 1], P),
                              ALU.mult).then_inc(a_vn1, 1)
            dve.wait_ge(a_ors, g + 1)
            o_ = qkv[:, bass.ds(4 * g + 16, 4), :]
            link(dve.tensor_tensor(o_, banks(2, 2).rearrange("p (h b) i -> p h (b i)", b=2), sq[:, 4:8, :],
                                   ALU.mult))
            dve.tensor_tensor(o_, o_, z_gate[:, g4, :], ALU.mult).then_inc(a_free, 1)
        repeat(dve, GROUPS_A, group, link, 1)
        dve.wait_ge(a_free, GROUPS_A + 1)
        for half in range(2):
            k4 = slice(4 * half, 4 * half + 4)
            split_act(qkv[:, 16 + 4 * half:20 + 4 * half, :], o_hi[:, k4, :], o_lo[:, k4, :]).then_inc(a_osplit, 2)
        splits(3)

    att_scores, att_masked, att_max, att_exp, att_p = (
        sem(f"att_{n}") for n in ("scores", "masked", "max", "exp", "p"))
    att_turned, att_ptkept, att_o, att_out = (sem(f"att_{n}") for n in ("turned", "ptkept", "o", "out"))
    att_vturned, att_vtok, att_in = sem("att_vturned"), sem("att_vtok"), sem("att_in")

    def att_buffers(m, tag):
        return {"score": m.take(f"score_{tag}", [P, 2, 4, T]), "p_t": m.take(f"p_t_{tag}", [P, 2, 4, NB, P])}

    def att_pe(pe, groups, q, k, v_tok_, buf, base):
        def scores(n):
            g = groups[n]
            if n >= 2:
                pe.wait_ge(att_masked, base + n - 1)
            half = slice(64 * g["half"], 64 * g["half"] + 64)
            nk = g["keys"]
            for t in range(4):
                last = pe.matmul(M_ps[:, 2 * (n % 2) + t // 2, T * (t % 2):T * (t % 2) + nk],
                                 q[half, g["qt"] + t, P * g["blk"]:P * g["blk"] + P], k[half, g["kt"], 0:nk],
                                 start=True, stop=True)
            last.then_inc(att_scores, 1)
        scores(0)
        for n, g in enumerate(groups):
            if n + 1 < len(groups):
                scores(n + 1)
            pe.wait_ge(att_p, base + n + 1)
            if n:
                pe.wait_ge(att_ptkept, base + n)
            for t in range(4):
                for kb in range(g["keys"] // P):
                    c = (2 * t + kb) * P
                    last = pe.transpose(D_ps[:, c // 512, c % 512:c % 512 + P],
                                        buf["score"][:, n % 2, t, P * kb:P * kb + P], ident)
            last.then_inc(att_turned, 1)
            pe.wait_ge(att_ptkept, base + n + 1)
            if n >= 2:
                pe.wait_ge(att_out, base + n - 1)
            for t in range(4):
                for kb in range(g["keys"] // P):
                    last = pe.matmul(D_ps[64 * (t % 2):64 * (t % 2) + 64, 2 + n % 2, P * (t // 2):P * (t // 2) + P],
                                     v_tok_[:, g["vt"], kb, 64 * g["half"]:64 * g["half"] + 64],
                                     buf["p_t"][:, n % 2, t, kb, :], start=kb == 0, stop=kb == g["keys"] // P - 1)
            last.then_inc(att_o, 1)

    def att_act(act, groups, small_, buf, base):
        for n, g in enumerate(groups):
            act.wait_ge(att_max, base + n + 1)
            nk = g["keys"]
            for t in range(4):
                act.activation(buf["score"][:, n % 2, t, 0:nk], buf["score"][:, n % 2, t, 0:nk], ACT.Exp,
                               bias=small_[:, n, 1, t:t + 1], accum_out=small_[:, n, 3, t:t + 1])
            act.activation(small_[:, n, 2, :], small_[:, n, 2, :], ACT.Exp).then_inc(att_exp, 1)
            act.wait_ge(att_turned, base + n + 1)
            keep = slice(0, nk // P)
            act.activation(buf["p_t"][:, n % 2, :, keep, :],
                           D_ps[:, 0:2, :].rearrange("p b (t k q) -> p (b t) k q", t=2, k=NB)[:, :, keep, :],
                           ACT.Copy).then_inc(att_ptkept, 1)

    def att_dve(dve, link, groups, small_, buf, sink, o_hi_, o_lo_, split_act, base):
        def masked(n):
            g = groups[n]
            nk = g["keys"]
            dve.wait_ge(att_scores, base + n + 1)
            if n >= 2:
                dve.wait_ge(att_turned, base + n - 1)
            sc = buf["score"][:, n % 2, :, 0:nk]
            dve.scalar_tensor_tensor(out=sc, in0=M_ps[:, 2 * (n % 2):2 * (n % 2) + 2, :]
                                     .rearrange("p b (t k) -> p (b t) k", t=2)[:, :, 0:nk], scalar=0.125,
                                     in1=over_mid(g["mask"], 4), op0=ALU.mult, op1=ALU.add).then_inc(att_masked, 1)
            dve.wait_ge(att_masked, base + n + 1)
            link(dve.reduce_max(small_[:, n, 0, :], sc, AX.X))
            link(dve.tensor_tensor(small_[:, n, 0, :], small_[:, n, 0, :], sink(g), ALU.max))
            dve.tensor_scalar(small_[:, n, 1, :], small_[:, n, 0, :], -1.0, None, ALU.mult)
            dve.tensor_tensor(small_[:, n, 2, :], sink(g), small_[:, n, 0, :], ALU.subtract).then_inc(att_max, 1)
        masked(0)
        for n, g in enumerate(groups):
            if n + 1 < len(groups):
                masked(n + 1)
            nk = g["keys"]
            dve.wait_ge(att_exp, base + n + 1)
            link(dve.tensor_tensor(small_[:, n, 3, :], small_[:, n, 3, :], small_[:, n, 2, :], ALU.add))
            link(dve.reciprocal(small_[:, n, 4, :], small_[:, n, 3, :]))
            sc = buf["score"][:, n % 2, :, 0:nk]
            dve.tensor_tensor(sc, sc, over_free(small_[:, n, 4, :], nk), ALU.mult).then_inc(att_p, 1)
            dve.wait_ge(att_o, base + n + 1)
            o_ = D_ps[:, 2 + n % 2, 0:2 * P].rearrange("p (k t) -> p k t", t=P)
            k2, t_ = slice(g["ot"], g["ot"] + 2), slice(P * g["blk"], P * g["blk"] + P)
            split_act(o_, o_hi_[:, k2, t_], o_lo_[:, k2, t_]).then_inc(att_out, 1)

    m = Map(nc, arena, end)
    qkv_b = m.take("qkv_b", [P, 12, T])
    ao_hi_b = m.take("ao_hi_b", [P, 8, T], F32R)
    ao_lo_b = m.take("ao_lo_b", [P, 8, T], F32R)
    buf_b = att_buffers(m, "b")
    v_tok_b = m.take("v_tok_b", [P, 2, NB, P])
    small_b = m.take("small_b", [P, 8, 5, 4])
    groups_b = [{"qt": 4 * c, "half": s_, "blk": b, "kt": 8 + c, "vt": c, "keys": P * (b + 1),
                 "mask": constant("band_prev")[:, P:T] if b == 0 else constant("band_prev"),
                 "ot": 2 * (2 * c + s_), "sink": 16 + 4 * (2 * c + s_)}
                for c in range(2) for b in range(NB) for s_ in range(2)]

    def mixer_b_pe(pe, run_narrow, wide):
        run_narrow("b_in")
        pe.wait_ge(dense_drained, 2 + FILL_OF["b_in"] + 3)
        for u in range(2):
            for b in range(NB):
                last = pe.transpose(D_ps[:, 3, P * (2 * u + b):P * (2 * u + b) + P],
                                    qkv_b[:, 10 + u, P * b:P * b + P], ident)
        last.then_inc(att_vturned, 1)
        pe.wait_ge(att_vtok, 1)
        att_pe(pe, groups_b, qkv_b, qkv_b, v_tok_b, buf_b, 0)
        pe.wait_ge(att_out, len(groups_b))
        wide("b_out", ao_hi_b, ao_lo_b)

    def mixer_b_act(act, link, narrow, splits):
        narrow("b_in", lambda c, q: None)
        att_act(act, groups_b, small_b, buf_b, 0)
        splits(3)

    def mixer_b_dve(dve, link, narrow, splits, split_act, before_norm):
        f0 = FILL_OF["b_in"]

        def body(c, q):
            for i in range(4):
                ps = D_ps[:, 2 * ((f0 + q) % 2) + i // 2, T * (i % 2):T * (i % 2) + T]
                last = dve.tensor_scalar(qkv_b[:, 4 * c + i, :], ps, column("b_b_in", 4 * c + i), None, ALU.add)
            last.then_inc(dense_drained, 1)
        narrow("b_in", body)
        dve.wait_ge(att_vturned, 1)
        dve.tensor_copy(v_tok_b[:, :, :, :], D_ps[:, 3, :].rearrange("p (u b i) -> p u b i", u=2, b=2)).then_inc(att_vtok, 1)
        att_dve(dve, link, groups_b, small_b, buf_b, lambda g: bcast[:, g["sink"]:g["sink"] + 4], ao_hi_b, ao_lo_b,
                split_act, 0)
        splits(3)
        f0 = FILL_OF["b_out"]
        for e in range(2):
            wait_half(dve, "b_out", e)
            for k in range(4):
                ps = D_ps[:, 2 * ((f0 + e) % 2) + k // 2, T * (k % 2):T * (k % 2) + T]
                last = dve.scalar_tensor_tensor(out=xT[:, 4 * e + k, :], in0=ps, scalar=column("b_b_out", 4 * e + k),
                                                in1=xT[:, 4 * e + k, :], op0=ALU.add, op1=ALU.add)
            last.then_inc(dense_drained, 1)
            if "ffn3" in STAGES:
                before_norm("ffn3", e)
        splits(1)

    m = Map(nc, arena, end)
    gts = m.take("gts", [P, 16, T])
    zs = m.take("zs", [P, ZT, T])
    gg = m.take("gg", [P, 4, T])
    ao_hi_c = m.take("ao_hi_c", [P, 4, T], F32R)
    ao_lo_c = m.take("ao_lo_c", [P, 4, T], F32R)
    at = m.at
    l_dec = m.take("l_dec", [P, 2, 4, T])
    a_lr = m.take("a_lr", [P, 2, 4, T])
    at2 = m.at
    m.at = at
    buf_c = att_buffers(m, "c")
    m.at = at2
    small_r = m.take("small_r", [P, 64])
    neg_bias = m.take("neg_bias", [P, 16])
    at = m.at
    zp = m.take("zp", [P, ZT, T + 2])
    qk = m.take("qk", [P, 5, T])
    v_c = m.take("v_c", [P, 1, T])
    lora = m.take("lora", [P, 2, 4 * P])
    g2w = m.take("g2w", [P, 4 * P])
    v_tok_c = m.take("v_tok_c", [P, 1, NB, P])
    small_c = m.take("small_c", [P, 4, 5, 4])
    m.at = at
    x_r = m.take("x_r", [P, 8, P])
    xt_r = m.take("xt_r", [P, 8, P])
    ly_r = m.take("ly_r", [P, 8, P])
    ar = m.take("ar", [P, 2, NB, 2, P])
    bk = m.take("bk", [P, 2, 2, NB, P])
    bk_tok = m.take("bk_tok", [P, 2, 2, P])
    v_tok_r = m.take("v_tok_r", [P, NB, P])
    w_sys = m.take("w_sys", [P, 4, P])
    u_tok = m.take("u_tok", [P, 2, 2, P])
    s_bd = m.take("s_bd", [P, 2, P])
    v_r = m.take("v_r", [P, T])
    m = Map(nc, h_at, arena)
    gram = m.take("gram", [P, 8, 4 * P])
    m = Map(nc, scratch_at, h_at)
    pq = m.take("pq", [P, 2, 2, T])
    e3 = m.take("e3", [P, 2, 3, T])
    kk = m.take("kk", [P, T])
    kk_rs = m.take("kk_rs", [P, T])
    kd = m.take("kd", [P, T])
    ba = m.take("ba", [P, T])
    bonus = m.take("bonus", [P, T])
    y_c = pq[:, 0, 0, :]
    y_n = pq[:, 0, 1, :]
    y_sq = pq[:, 1, 0, :]
    bn = pq[:, 1, 1, :]
    m = Map(nc, arena + 16 * T * 4, end)
    merged = m.take("merged", [P, KD, T])
    branch = m.take("branch", [P, KD, T])
    mg_hi = m.take("mg_hi", [P, KD, T], F32R)
    mg_lo = m.take("mg_lo", [P, KD, T], F32R)
    rw_hi = m.take("rw_hi", [P, 4, T], F32R)
    rw_lo = m.take("rw_lo", [P, 4, T], F32R)
    m = Map(nc, arena, end)
    ple_out = m.take("ple_out", [P, KD, T])
    ple_gate = m.take("ple_gate", [P, KD, T])
    groups_c = [{"qt": 0, "half": s_, "blk": b, "kt": 4, "vt": 0, "keys": T,
                 "mask": constant("band_first") if b == 0 else constant("band_last"),
                 "ot": 2 * s_, "sink": 32 + 4 * s_} for b in range(NB) for s_ in range(2)]
    SQRT_E = float(np.exp(-0.5))

    lora_loaded = sem("lora_loaded")
    c_edge, c_gate = sem("c_edge"), sem("c_gate")
    c_sq, c_ss, c_rs, c_qk, c_rot, c_qkv, c_vturn = (sem(f"c_{n}") for n in ("sq", "ss", "rs", "qk", "rot", "qkv", "vturn"))
    c_sum, c_shift, c_tanh, c_rank, c_lora, c_lexp, c_g = (sem(f"c_{n}") for n in (
        "sum", "shift", "tanh", "rank", "lora", "lexp", "g"))
    (r_free, r_kk0, r_sqk, r_v, r_ssk, r_vtok, r_ssm, r_rk, r_pq, r_ex, r_ops, r_bkt, r_bktok, r_bonus, r_bv, r_grm,
     r_g, r_init) = (sem(f"r_{n}") for n in (
         "free", "kk0", "sqk", "v", "ssk", "vtok", "ssm", "rk", "pq", "ex", "ops", "bkt", "bktok", "bonus", "bv",
         "gram", "g", "init"))
    r_w, r_wk, r_u, r_uk, r_s, r_sk, r_y, r_yk, r_mu, r_yc, r_ysq, r_var, r_rv, r_split = (sem(f"r_{n}") for n in (
        "w", "wk", "u", "uk", "s", "sk", "y", "yk", "mu", "yc", "ysq", "var", "rv", "split"))
    m_ready, p_gate = sem("m_ready"), sem("p_gate")
    NEED_R = ((2, 4), (0, 2))

    def load_lora(act):
        act.wait_ge(x_ready, 2)
        act.dma_start(lora[0:64, :, :], A["w2_2"][0].rearrange("d r c -> r d c")).then_inc(lora_loaded, 16)
        act.dma_start(lora[64:128, :, :], A["a2_2"][0].rearrange("d r c -> r d c")).then_inc(lora_loaded, 16)
        act.dma_start(g2w[:, :], A["g2_2"][0]).then_inc(lora_loaded, 16)

    def hybrid_pe(pe, run_narrow, wide):
        run_narrow("in2")
        pe.wait_ge(dense_drained, 2 + FILL_OF["in2"] + COUNT_OF["in2"])
        spans = [(0, 2), (2, 4), (4, 5)]

        def five(lhs, rhs):
            for i, (a, b) in enumerate(spans):
                last = pe.matmul(M_ps[:, i, 0:T * (b - a)], lhs, rhs[:, a:b, :].rearrange("p k t -> p (k t)"),
                                 start=True, stop=True)
            return last
        pe.wait_ge(c_sq, 1)
        five(ones_head, sq).then_inc(c_ss, 1)
        pe.wait_ge(c_qk, 1)
        five(constant("rotate"), qk).then_inc(c_rot, 1)
        for b in range(NB):
            last = pe.transpose(M_ps[:, 3, P * b:P * b + P], v_c[:, 0, P * b:P * b + P], ident)
        last.then_inc(c_vturn, 1)
        pe.wait_ge(c_qkv, 1)
        att_pe(pe, groups_c, qk, qk, v_tok_c, buf_c, len(groups_b))
        pe.wait_ge(att_out, len(groups_b) + len(groups_c))
        pe.wait_ge(lora_loaded, 48)
        pe.wait_ge(c_rank, 1)
        for d in range(2):
            for i in range(4):
                c = 4 * d + i
                for half, bank in ((0, M_ps), (1, D_ps)):
                    p_ = slice(64 * half, 64 * half + 64)
                    last = pe.matmul(bank[:, c // 2, T * (c % 2):T * (c % 2) + T], lora[p_, d, P * i:P * i + P],
                                     zs[p_, 12, :], start=True, stop=True)
        last.then_inc(c_lora, 1)
        pe.wait_ge(c_lexp, 1)
        for i in range(4):
            last = pe.matmul(M_ps[:, i // 2, T * (i % 2):T * (i % 2) + T], g2w[:, P * i:P * i + P], zs[:, 13, :],
                             start=True, stop=True)
        last.then_inc(c_lora, 1)

        def bank_of(s_):
            return (M_ps if s_ < 4 else D_ps)[:, s_ % 4, :]

        def tile(i):
            pe.wait_ge(r_free, i + 1)
            pe.wait_ge(r_sqk, i + 1)
            pe.matmul(M_ps[:, 0, 0:T], ones_head, kk_rs[:, :], start=True, stop=True).then_inc(r_ssk, 1)
            pe.wait_ge(r_v, i + 1)
            for b in range(NB):
                last = pe.transpose(M_ps[:, 1, P * b:P * b + P], v_r[:, P * b:P * b + P], ident)
            last.then_inc(r_ssk, 1)
            pe.wait_ge(r_vtok, i + 1)
            pe.wait_ge(r_ops, i + 1)
            for d in range(2):
                for x in range(2):
                    last = pe.transpose(M_ps[:, 1, P * (2 * d + x):P * (2 * d + x) + P], bk[:, d, x, d, :], ident)
            last.then_inc(r_bkt, 1)
            pe.matmul(M_ps[:, 0, 0:T], ones_head, bn, start=True, stop=True).then_inc(r_bonus, 1)
            pe.wait_ge(r_bktok, i + 1)
            pe.wait_ge(r_bv, i + 1)
            for h in range(2):
                p_ = slice(64 * h, 64 * h + 64)
                for d in range(2):
                    for b in range(NB):
                        o_ = bank_of(4 * h + 2 * d + b)
                        a_r = ar[p_, d, b, :, :].rearrange("p x t -> p (x t)")
                        if d == 0:
                            pe.matmul(o_[:, 0:2 * P], bk[p_, d, 0, b, :], a_r, start=True, stop=True)
                        else:
                            pe.matmul(o_[:, 0:P], ar[p_, d, b, 0, :], bk[p_, d, 0, b, :], start=True, stop=True)
                            pe.matmul(o_[:, P:2 * P], bk[p_, d, 0, b, :], ar[p_, d, b, 1, :], start=True, stop=True)
                        last = pe.matmul(o_[:, 2 * P:4 * P], bk[p_, d, 1, b, :], a_r, start=True, stop=True)
                last.then_inc(r_grm, 1)
            inverse_pe(pe, lambda s_: gram[:, s_, 0:P], x_r, xt_r, ly_r, [(r_g, 2 * i + 2), (r_init, i + 1)],
                       GROUPS_A + i, NEED_R)
            for half in range(2):
                pe.wait_ge(inv_up, 14 * (GROUPS_A + i) + 13 + half)

            def apply(d, s_):
                return (xt_r, x_r)[d][:, s_, :]
            for phase in range(2):
                first = phase == 0
                if not first:
                    pe.wait_ge(r_sk, i + 1)
                for h in range(2):
                    for d in range(2):
                        b = d if first else 1 - d
                        s_ = 4 * h + 2 * d + b
                        o_ = M_ps[:, 0, P * (2 * h + d):P * (2 * h + d) + P]
                        last = pe.matmul(o_, gram[:, s_, 2 * P:3 * P], v_tok_r[:, b, :], start=True, stop=first)
                        if not first:
                            last = pe.matmul(o_, ar[:, d, b, 0, :], s_bd[:, d, :], start=False, stop=True)
                last.then_inc(r_w, 1)
                pe.wait_ge(r_wk, 2 * i + phase + 1)
                for h in range(2):
                    for d in range(2):
                        b = d if first else 1 - d
                        last = pe.matmul(M_ps[:, 1, P * (2 * h + d):P * (2 * h + d) + P], apply(d, 4 * h + 2 * d + b),
                                         w_sys[:, 2 * h + d, :], start=True, stop=True)
                last.then_inc(r_u, 1)
                pe.wait_ge(r_uk, 2 * i + phase + 1)
                if first:
                    for d in range(2):
                        o_ = M_ps[:, 2, P * d:P * d + P]
                        pe.matmul(o_, bk_tok[:, d, 0, :], u_tok[:, 0, d, :], start=True, stop=False)
                        last = pe.matmul(o_, bk_tok[:, d, 1, :], v_tok_r[:, d, :], start=False, stop=True)
                    last.then_inc(r_s, 1)
            for b in range(NB):
                o_ = M_ps[:, 3, P * b:P * b + P]
                pe.matmul(o_, s_bd[:, 1 - b, :], ar[:, 1 - b, b, 1, :], start=True, stop=False)
                for d in range(2):
                    for h in range(2):
                        s_ = 4 * h + 2 * d + b
                        p_ = slice(64 * h, 64 * h + 64)
                        pe.matmul(o_[p_, :], u_tok[:, 0 if b == d else 1, d, p_], gram[:, s_, P:2 * P],
                                  start=False, stop=False)
                        last = pe.matmul(o_[p_, :], v_tok_r[:, b, p_], gram[:, s_, 3 * P:4 * P],
                                         start=False, stop=d == 1)
            last.then_inc(r_y, 1)
            pe.wait_ge(r_yk, i + 1)
            pe.matmul(M_ps[:, 0, 0:T], ones_head, y_n, start=True, stop=True).then_inc(r_mu, 1)
            pe.wait_ge(r_ysq, i + 1)
            pe.matmul(M_ps[:, 1, 0:T], ones_head, y_sq, start=True, stop=True).then_inc(r_var, 1)
        repeat(pe, 4, tile)
        wide("up_attn", ao_hi_c, ao_lo_c)
        wide("up_rwkv", rw_hi, rw_lo, (r_split, 0))
        wide("out2", mg_hi, mg_lo, (m_ready, 0))

    def hybrid_pool(pool):
        pool.wait_ge(x_ready, 2)
        pool.memset(zp[:, :, 0:1], 0.0)
        pool.memset(zp[:, :, T + 1:T + 2], 0.0).then_inc(c_edge, 1)
        pool.wait_ge(c_edge, 1)
        pool.wait_ge(dense_drained, 2 + FILL_OF["in2"] + 5)
        pool.tensor_tensor(zs[:, :, :], zp[:, :, 0:T], zp[:, :, 2:T + 2], ALU.add).then_inc(c_sum, 1)
        pool.wait_ge(piece_used, PIECE_OF["in2"] + 2 * COUNT_OF["in2"])
        pool.memset(gram[:, :, :], 0.0).then_inc(c_edge, 1)

        def tile(i):
            pool.wait_ge(r_free, i + 1)
            alone(pool)
            pool.tensor_copy(x_r[:, :, :], over_mid(ident, 8))
            pool.tensor_copy(xt_r[:, :, :], over_mid(ident, 8)).then_inc(r_init, 1)
        repeat(pool, 4, tile)

    def hybrid_act(act, link, narrow, splits):
        load_lora(act)
        f0 = FILL_OF["in2"]
        narrow("in2", lambda c, q: None, 0, 0, 4)
        narrow("in2", lambda c, q: None, 0, 4, 1)

        def gates_(c, q):
            ps = D_ps[:, 2 * ((f0 + 1 + q) % 2):2 * ((f0 + 1 + q) % 2) + 2, :].rearrange("p a (k t) -> p (a k) t", t=T)
            alone(act)
            act.activation(gts[:, bass.ds(4 * c, 4), :], ps, ACT.Sigmoid).then_inc(c_gate, 1)
        act.preload_act_table(ACT.Sigmoid)
        narrow("in2", gates_, 0, 5, 4)
        act.preload_act_table_set(LN_EXP)
        act.activation(sq[:, 0:5, :], qk[:, :, :], ACT.Square).then_inc(c_sq, 1)
        act.wait_ge(c_ss, 1)
        for i, (a, b) in enumerate([(0, 2), (2, 4), (4, 5)]):
            last = act.activation(sq[:, a:b, :].rearrange("p k t -> p (k t)"), M_ps[:, i, 0:T * (b - a)], ACT.Ln,
                                  bias=eps_col, scale=1.0 / 64)
        link(last)
        act.activation(sq[:, 0:5, :], sq[:, 0:5, :], ACT.Exp, scale=-0.5).then_inc(c_rs, 1)
        act.wait_ge(c_shift, 1)
        act.activation(zs[0:64, 12, :], zs[0:64, 12, :], ACT.Exp, scale=-2.0)
        act.activation(zs[:, 13, :], zs[:, 13, :], ACT.Exp, scale=-1.0).then_inc(c_tanh, 1)
        att_act(act, groups_c, small_c, buf_c, len(groups_b))
        act.wait_ge(c_lora, 1)
        for d in range(2):
            for i in range(4):
                c = 4 * d + i
                for which, (dst, bank) in enumerate(((l_dec, M_ps), (a_lr, D_ps))):
                    last = act.activation(dst[:, d, i, :], bank[:, c // 2, T * (c % 2):T * (c % 2) + T], ACT.Exp,
                                          bias=neg_bias[:, 8 * which + c:8 * which + c + 1], scale=-1.0)
        last.then_inc(c_lexp, 1)
        act.wait_ge(c_lora, 2)
        act.activation(gg[:, :, :], M_ps[:, 0:2, :].rearrange("p b (k t) -> p (b k) t", t=T), ACT.Copy).then_inc(c_g, 1)

        def tile(i):
            act.wait_ge(r_free, i + 1)
            alone(act)
            act.activation(v_r[:, :], zs[:, bass.ds(8 + i, 1), :].rearrange("p a t -> p (a t)"), ACT.Copy).then_inc(r_v, 1)
            act.wait_ge(r_kk0, i + 1)
            act.activation(kk_rs[:, :], kk[:, :], ACT.Square).then_inc(r_sqk, 1)
            act.wait_ge(r_ssk, 2 * i + 2)
            act.activation(v_tok_r[:, :, :], M_ps[:, 1, 0:T].rearrange("p (b i) -> p b i", i=P), ACT.Copy).then_inc(r_vtok, 1)
            act.wait_ge(r_ssm, i + 1)
            link(act.activation(kk_rs[:, :], kk_rs[:, :], ACT.Ln, scale=2.0 ** 24))
            act.activation(kk_rs[:, :], kk_rs[:, :], ACT.Exp, scale=-0.5,
                           bias=cst[:, CONST_AT["tiny"][0] + 2:CONST_AT["tiny"][0] + 3]).then_inc(r_rk, 1)
            act.wait_ge(r_pq, i + 1)
            for d, j, src, sign in ((0, 0, 0, 1.0), (0, 1, 1, 1.0), (0, 2, 0, -1.0),
                                    (1, 0, 1, -1.0), (1, 1, 0, -1.0), (1, 2, 1, 1.0)):
                act.activation(e3[:, d, j, :], pq[:, d, src, :], ACT.Exp, scale=sign)
            act.activation(small_r[:, 8:10], small_r[:, 8:10], ACT.Exp, scale=-1.0).then_inc(r_ex, 1)
            act.wait_ge(r_bkt, i + 1)
            act.activation(bk_tok[:, :, :, :], M_ps[:, 1, :].rearrange("p (d x i) -> p d x i", d=2, x=2),
                           ACT.Copy).then_inc(r_bktok, 1)
            inverse_act(act, ly_r, GROUPS_A + i)
            for phase in range(2):
                act.wait_ge(r_w, 2 * i + phase + 1)
                act.activation(w_sys[:, :, :], banks(0, 1), ACT.Copy).then_inc(r_wk, 1)
            act.wait_ge(r_y, i + 1)
            act.activation(y_n, M_ps[:, 3, 0:T], ACT.Copy).then_inc(r_yk, 1)
            act.wait_ge(r_yc, i + 1)
            act.activation(y_sq, y_c, ACT.Square).then_inc(r_ysq, 1)
            act.wait_ge(r_var, i + 1)
            link(act.activation(kk_rs[:, :], M_ps[:, 1, 0:T], ACT.Ln, scale=1.0 / 64,
                                bias=cst[:, CONST_AT["tiny"][0] + 1:CONST_AT["tiny"][0] + 2]))
            act.activation(kk_rs[:, :], kk_rs[:, :], ACT.Exp, scale=-0.5).then_inc(r_rv, 1)
        repeat(act, 4, tile, link, 2)
        splits(7)

    def hybrid_dve(dve, link, narrow, splits, split_act):
        f0 = FILL_OF["in2"]

        def keep(c, q):
            ps = D_ps[:, 2 * ((f0 + q) % 2):2 * ((f0 + q) % 2) + 2, :].rearrange("p a (k t) -> p (a k) t", t=T)
            if c == 0:
                dve.tensor_copy(qk[:, 0:4, :], ps).then_inc(dense_drained, 1)
            elif c == 1:
                dve.tensor_copy(qk[:, 4, :], ps[:, 0, :])
                dve.tensor_copy(v_c[:, 0, :], ps[:, 1, :])
                dve.tensor_copy(zp[:, 0:2, 1:T + 1], ps[:, 2:4, :]).then_inc(dense_drained, 1)
            else:
                dve.tensor_copy(zp[:, 4 * c - 6:4 * c - 2, 1:T + 1], ps).then_inc(dense_drained, 1)
        narrow("in2", keep, 0, 0, 2)
        narrow("in2", lambda c, q: keep(c + 2, q), 0, 2, 2)
        narrow("in2", lambda c, q: keep(c + 4, q), 0, 4, 1)


        def gates_(c, q):
            dve.wait_ge(c_gate, c + 1)
            dve.wait_ge(dense_drained, 2 + f0 + 5 + c)
            dve.nop().then_inc(dense_drained, 1)
        narrow("in2", gates_, 0, 5, 4)
        dve.wait_ge(c_sum, 1)
        zc = zp[:, :, 1:T + 1]
        link(dve.scalar_tensor_tensor(out=zs[:, :, :], in0=zs[:, :, :], scalar=0.5, in1=zc, op0=ALU.mult,
                                      op1=ALU.subtract))
        for i in range(ZT):
            last = dve.scalar_tensor_tensor(out=zs[:, i, :], in0=zs[:, i, :], scalar=column("shift_mu_2", i),
                                            in1=zp[:, i, 1:T + 1], op0=ALU.mult, op1=ALU.add)
        last.then_inc(c_shift, 1)
        dve.tensor_scalar(neg_bias[:, 0:8], cols[:, P + ROWS_B["w0_2"][0]:P + ROWS_B["w0_2"][0] + 8], -1.0, None,
                          ALU.mult)
        dve.tensor_scalar(neg_bias[:, 8:16], cols[:, P + ROWS_B["a0_2"][0]:P + ROWS_B["a0_2"][0] + 8], -1.0, None,
                          ALU.mult)
        dve.wait_ge(c_tanh, 1)
        th, sg = zs[0:64, 12, :], zs[:, 13, :]
        dve.tensor_scalar(sg, sg, 1.0, None, ALU.add)
        link(dve.tensor_scalar(th, th, 1.0, None, ALU.add))
        dve.reciprocal(sg, sg)
        link(dve.reciprocal(th, th))
        dve.tensor_scalar(th, th, 2.0, -1.0, ALU.mult, ALU.add).then_inc(c_rank, 1)
        dve.wait_ge(c_rs, 1)
        dve.scalar_tensor_tensor(out=qk[:, 0:4, :], in0=qk[:, 0:4, :], scalar=column("q_norm_2"), in1=sq[:, 0:4, :],
                                 op0=ALU.mult, op1=ALU.mult)
        dve.scalar_tensor_tensor(out=qk[:, 4, :], in0=qk[:, 4, :], scalar=column("k_norm_2"), in1=sq[:, 4, :],
                                 op0=ALU.mult, op1=ALU.mult).then_inc(c_qk, 1)
        dve.wait_ge(c_rot, 1)
        for i, (a, b) in enumerate([(0, 2), (2, 4), (4, 5)]):
            dve.tensor_tensor(sq[:, a:b, :], M_ps[:, i, 0:T * (b - a)].rearrange("p (k t) -> p k t", t=T),
                              over_mid(constant("sin"), b - a), ALU.mult)
        link(dve.tensor_tensor(qk[:, :, :], qk[:, :, :], over_mid(constant("cos"), 5), ALU.mult))
        dve.tensor_tensor(qk[:, :, :], qk[:, :, :], sq[:, 0:5, :], ALU.add)
        dve.wait_ge(c_vturn, 1)
        dve.tensor_copy(v_tok_c[:, 0, :, :], M_ps[:, 3, 0:T].rearrange("p (b i) -> p b i", i=P)).then_inc(c_qkv, 1)
        att_dve(dve, link, groups_c, small_c, buf_c, lambda g: bcast[:, g["sink"]:g["sink"] + 4], ao_hi_c, ao_lo_c,
                split_act, len(groups_b))
        dve.wait_ge(c_lexp, 1)
        dve.tensor_scalar(l_dec[:, :, :, :], l_dec[:, :, :, :], 1.0, None, ALU.add)
        link(dve.tensor_scalar(a_lr[:, :, :, :], a_lr[:, :, :, :], 1.0, None, ALU.add))
        dve.reciprocal(a_lr[:, :, :, :], a_lr[:, :, :, :])
        link(dve.reciprocal(l_dec[:, :, :, :], l_dec[:, :, :, :]))
        link(dve.tensor_scalar(l_dec[:, :, :, :], l_dec[:, :, :, :], -SQRT_E, None, ALU.mult))
        dve.wait_ge(c_g, 1)
        dve.wait_ge(c_edge, 2)
        dve.nop().then_inc(r_free, 1)

        def tile(i):
            def z(k):
                return zs[:, bass.ds(4 * k + i, 1), :].rearrange("p a t -> p (a t)")

            def col(name, k=0):
                at = ROWS_A[name][0] if name in ROWS_A else P + ROWS_B[name][0]
                return cols[:, bass.ds(at + 4 * k + i, 1)]

            def by_chunk(ap):
                return ap.rearrange("p (b t) -> p b t", t=P)
            dve.tensor_scalar(kk[:, :], z(1), col("k_k_2"), None, ALU.mult).then_inc(r_kk0, 1)
            tot, mid = small_r[:, 0:4], small_r[:, 4:8]
            for d in range(2):
                last = dve.tensor_reduce(tot[:, 2 * d:2 * d + 2],
                                         l_dec[:, d, bass.ds(i, 1), :].rearrange("p a (b t) -> p (a b) t", t=P),
                                         AX.X, ALU.add)
            link(last)
            link(dve.tensor_scalar(mid, tot, -0.5, None, ALU.mult))
            dve.tensor_tensor(small_r[:, 8:10], mid.rearrange("p (d b) -> p d b", b=2)[:, :, 0],
                              mid.rearrange("p (d b) -> p d b", b=2)[:, :, 1], ALU.add)
            for d in range(2):
                for b in range(NB):
                    l_ = l_dec[:, d, bass.ds(i, 1), P * b:P * b + P].rearrange("p a t -> p (a t)")
                    last = dve.tensor_tensor_scan(pq[:, d, 0, P * b:P * b + P], ones, l_,
                                                  mid[:, 2 * d + b:2 * d + b + 1], ALU.mult, ALU.add)
            link(last)
            for d in range(2):
                l_ = l_dec[:, d, bass.ds(i, 1), :].rearrange("p a t -> p (a t)")
                last = dve.tensor_tensor(pq[:, d, 1, :], pq[:, d, 0, :], l_, ALU.subtract)
            last.then_inc(r_pq, 1)
            dve.wait_ge(r_ssk, 2 * i + 1)
            dve.wait_ge(r_sqk, i + 1)
            dve.tensor_scalar(kk_rs[:, :], M_ps[:, 0, 0:T], 1e-24, None, ALU.max).then_inc(r_ssm, 1)
            dve.wait_ge(r_rk, i + 1)
            link(dve.tensor_tensor(kk[:, :], kk[:, :], kk_rs[:, :], ALU.mult))
            dve.wait_ge(r_ex, i + 1)
            for d in range(2):
                a_ = a_lr[:, d, bass.ds(i, 1), :].rearrange("p a t -> p (a t)")
                link(dve.tensor_scalar(kd[:, :], a_, 1.0, col("k_a_2"), ALU.subtract, ALU.mult))
                dve.tensor_tensor(ba[:, :], kk[:, :], a_, ALU.mult)
                link(dve.scalar_tensor_tensor(out=kd[:, :], in0=kd[:, :], scalar=1.0, in1=z(1), op0=ALU.add,
                                              op1=ALU.mult))
                dve.scalar_tensor_tensor(out=ar[:, d, :, 0, :], in0=by_chunk(kk[:, :]), scalar=-1.0,
                                         in1=by_chunk(e3[:, d, 1, :]), op0=ALU.mult, op1=ALU.mult)
                dve.tensor_tensor(ar[:, d, :, 1, :], zs[:, bass.ds(i, 1), :].rearrange("p a (b t) -> p (a b) t", t=P),
                                  by_chunk(e3[:, d, 0, :]), ALU.mult)
                dve.tensor_tensor(bk[:, d, 0, :, :], by_chunk(ba[:, :]), by_chunk(e3[:, d, 2, :]), ALU.mult)
                dve.tensor_tensor(bk[:, d, 1, :, :], by_chunk(kd[:, :]), by_chunk(e3[:, d, 2, :]), ALU.mult)
                r_k = col("r_k_2", d)
                if d == 0:
                    link(dve.scalar_tensor_tensor(out=bn, in0=kd[:, :], scalar=r_k, in1=z(0), op0=ALU.mult,
                                                  op1=ALU.mult))
                else:
                    link(dve.scalar_tensor_tensor(out=kd[:, :], in0=kd[:, :], scalar=r_k, in1=z(0), op0=ALU.mult,
                                                  op1=ALU.mult))
                    dve.tensor_tensor(bn, bn, kd[:, :], ALU.add).then_inc(r_ops, 1)
            dve.wait_ge(r_bonus, i + 1)
            dve.tensor_tensor(bonus[:, :], M_ps[:, 0, 0:T], z(2), ALU.mult).then_inc(r_bv, 1)
            for h in range(2):
                dve.wait_ge(r_grm, 2 * i + h + 1)
                alone(dve)
                for s4 in range(4):
                    mask = mask8("mask_fwd") if s4 < 2 else mask8("mask_bwd")
                    last = dve.copy_predicated(out=gram[:, 4 * h + s4, :], mask=mask,
                                               data=(M_ps if h == 0 else D_ps)[:, s4, :])
                last.then_inc(r_g, 1)
            dve.wait_ge(r_init, i + 1)
            inverse_dve(dve, lambda half: gram[:, 4 * half:4 * half + 4, 0:P], x_r, xt_r, GROUPS_A + i, NEED_R)
            for phase in range(2):
                dve.wait_ge(r_u, 2 * i + phase + 1)
                u_ = banks(1, 1).rearrange("p (h d) i -> p h d i", h=2)
                dve.tensor_copy(u_tok[:, phase, :, 0:64], u_[:, 0, :, 0:64])
                dve.tensor_copy(u_tok[:, phase, :, 64:128], u_[:, 1, :, 64:128]).then_inc(r_uk, 1)
                if phase == 0:
                    dve.wait_ge(r_s, i + 1)
                    for d in range(2):
                        last = dve.scalar_tensor_tensor(out=s_bd[:, d, :], in0=M_ps[:, 2, P * d:P * d + P],
                                                        scalar=small_r[:, 8 + d:9 + d], in1=ones_head,
                                                        op0=ALU.mult, op1=ALU.mult)
                    last.then_inc(r_sk, 1)
            dve.wait_ge(r_mu, i + 1)
            dve.scalar_tensor_tensor(out=y_c, in0=M_ps[:, 0, 0:T], scalar=-1.0 / 64, in1=y_n, op0=ALU.mult,
                                     op1=ALU.add).then_inc(r_yc, 1)
            dve.wait_ge(r_rv, i + 1)
            link(dve.scalar_tensor_tensor(out=y_n, in0=y_c, scalar=col("lnx_w_2"), in1=kk_rs[:, :], op0=ALU.mult,
                                          op1=ALU.mult))
            link(dve.scalar_tensor_tensor(out=y_n, in0=y_n, scalar=col("lnx_b_2"), in1=bonus[:, :], op0=ALU.add,
                                          op1=ALU.add))
            dve.tensor_tensor(z(0), y_n, gg[:, bass.ds(i, 1), :].rearrange("p a t -> p (a t)"),
                              ALU.mult).then_inc(r_free, 1)
        repeat(dve, 4, tile, link, 12)
        dve.wait_ge(r_free, 5)
        for k in range(2):
            k2 = slice(2 * k, 2 * k + 2)
            split_act(zs[:, k2, :], rw_hi[:, k2, :], rw_lo[:, k2, :]).then_inc(r_split, 1)
        dve.wait_ge(r_split, 2)
        splits(2)
        for job, which in (("up_attn", 0), ("up_rwkv", 1)):
            f0 = FILL_OF[job]
            dst = merged if which == 0 else branch
            for e in range(2):
                wait_half(dve, job, e)
                ps = D_ps[:, 2 * ((f0 + e) % 2):2 * ((f0 + e) % 2) + 2, :].rearrange("p a (k t) -> p (a k) t", t=T)
                k4 = slice(4 * e, 4 * e + 4)
                dve.tensor_tensor(dst[:, k4, :], ps, gts[:, 8 * which + 4 * e:8 * which + 4 * e + 4, :],
                                  ALU.mult).then_inc(dense_drained, 1)
            splits(2 if which == 0 else 0)
        dve.wait_ge(dense_drained, 2 + FILL_OF["up_rwkv"] + 2)
        for k in range(4):
            k2 = slice(2 * k, 2 * k + 2)
            link(dve.tensor_tensor(merged[:, k2, :], merged[:, k2, :], branch[:, k2, :], ALU.add))
            split_act(merged[:, k2, :], mg_hi[:, k2, :], mg_lo[:, k2, :]).then_inc(m_ready, 1)
        splits(3)

    def ple_act(act, link, splits):
        splits(5)
        f0 = FILL_OF["ple_gate"]
        for e in range(2):
            wait_half(act, "ple_gate", e)
            ps = D_ps[:, 2 * ((f0 + e) % 2):2 * ((f0 + e) % 2) + 2, :].rearrange("p a (k t) -> p (a k) t", t=T)
            act.activation(ple_gate[:, 4 * e:4 * e + 4, :], ps, ACT.Sigmoid).then_inc(p_gate, 1)

    def ple_dve(dve, link, splits, norm):
        f0 = FILL_OF["ple"]
        for e in range(2):
            wait_half(dve, "ple", e)
            ps = D_ps[:, 2 * ((f0 + e) % 2):2 * ((f0 + e) % 2) + 2, :].rearrange("p a (k t) -> p (a k) t", t=T)
            dve.tensor_copy(ple_out[:, 4 * e:4 * e + 4, :], ps).then_inc(dense_drained, 1)
        norm("ple")
        splits(4)
        for e in range(2):
            dve.wait_ge(p_gate, e + 1)
            k4 = slice(4 * e, 4 * e + 4)
            link(dve.tensor_tensor(ple_gate[:, k4, :], ple_gate[:, k4, :], ple_out[:, k4, :], ALU.mult))
            dve.tensor_tensor(xT[:, k4, :], xT[:, k4, :], ple_gate[:, k4, :], ALU.add).then_inc(x_final, 1)

    with nc.Block() as block:

        @block.sync
        def _(sp):
            def load_piece(p, src0, src1, turn=0):
                slot = p % RAW_SLOTS
                if p >= RAW_SLOTS:
                    sp.wait_ge(lo_ready, p - RAW_SLOTS + 1 + RAW_SLOTS * turn)
                half = PIECE // 2
                dst = raw[:, slot, :]
                if src0.shape[-1] == 2 * P:
                    v = dst.rearrange("p (k s n) -> p k s n", k=4, s=2)
                    d0, d1 = v[:, :, 0, :], v[:, :, 1, :]
                else:
                    d0, d1 = dst[:, 0:half], dst[:, half:]
                    if len(src0.shape) == 3:
                        d0 = d0.rearrange("p (k n) -> p k n", n=512)
                        d1 = d1.rearrange("p (k n) -> p k n", n=512)
                sp.dma_start(d0, src0).then_inc(raw_loaded[slot], 16)
                sp.dma_start(d1, src1).then_inc(raw_loaded[slot], 16)

            def load_gated(job):
                name, layer = gated[job]
                w = A[name][layer].rearrange("(k p) (s n) -> p k s n", p=P, s=2)
                p0 = PIECE_OF[job]

                def chunk(c, j, turn):
                    for r in range(2):
                        cols_ = w[:, 4 * r:4 * r + 4, :, bass.ds(c * 2 * P, 2 * P)]
                        load_piece(p0 + 2 * j + r, cols_[:, :, 0, :], cols_[:, :, 1, :], turn)
                first = 1 if p0 == 0 else 0
                if first:
                    chunk(0, 0, 0)
                    chunk(1, 1, 0)
                    sp.dma_start(mask_f32[:, :], A["masks"]).then_inc(mask_loaded, 16)
                n = COUNT_OF[job]
                whole = n // 2 - first

                def turn(t):
                    chunk(2 * t + 2 * first, 2 * first, t)
                    chunk(2 * t + 2 * first + 1, 2 * first + 1, t)
                repeat(sp, whole, turn)
                for c in range(2 * (whole + first), n):
                    chunk(c, c, 0)

            def load_narrow(job):
                w = A[others[job]][0].rearrange("(k p) n -> p k n", p=P)
                p0, n = PIECE_OF[job], COUNT_OF[job]

                def chunk(c, j, turn):
                    for r in range(2):
                        cols_ = w[:, 4 * r:4 * r + 4, bass.ds(c * 512, 512)]
                        load_piece(p0 + 2 * j + r, cols_[:, 0:2, :], cols_[:, 2:4, :], turn)

                def turn(t):
                    chunk(2 * t, 0, t)
                    chunk(2 * t + 1, 1, t)
                repeat(sp, n // 2, turn)
                for c in range(n // 2 * 2, n):
                    chunk(c, c, 0)

            def load_wide(job):
                name, layer = downs.get(job) or (others[job], 0)
                w = A[name][layer].rearrange("(k p) n -> k p n", p=P)
                p0, n = PIECE_OF[job], COUNT_OF[job]

                def turn(t):
                    for r in range(4):
                        k = 2 * r + 8 * t
                        load_piece(p0 + r, w[bass.ds(k, 1)].rearrange("a p n -> (a p) n"),
                                   w[bass.ds(k + 1, 1)].rearrange("a p n -> (a p) n"), t)
                repeat(sp, n // 4, turn)
                for r in range(n // 4 * 4, n):
                    load_piece(p0 + r, w[2 * r], w[2 * r + 1])

            def load_rows():
                def rows_of(name):
                    if name in ROWS_A:
                        return 0, *ROWS_A[name]
                    return 1, *ROWS_B[name]
                count = 0
                for name in list(ROWS_A) + list(ROWS_B):
                    which, at, n = rows_of(name)
                    if name == "b_b_in":
                        v = A[name][0, 0:1024].rearrange("(c s t d) -> c s t d", c=2, s=2, t=4)
                        for c in range(2):
                            for s in range(2):
                                sp.dma_start(rows[at + 4 * c:at + 4 * c + 4, which, 64 * s:64 * s + 64],
                                             v[c, s]).then_inc(in_loaded, 16)
                                count += 1
                        sp.dma_start(rows[at + 8:at + 12, which, :],
                                     A[name][0, 1024:1536].rearrange("(r e) -> r e", e=P)).then_inc(in_loaded, 16)
                        count += 1
                        continue
                    if name in ("q_norm_2", "k_norm_2"):
                        for s in range(2):
                            sp.dma_start(rows[at:at + 1, which, 64 * s:64 * s + 64], A[name]).then_inc(in_loaded, 16)
                            count += 1
                        continue
                    ap = A[name]
                    names = "abcd"[:len(ap.shape)]
                    flat = ap if len(ap.shape) == 1 else ap.rearrange(
                        " ".join(names) + " -> (" + " ".join(names) + ")")
                    sp.dma_start(rows[at:at + n, which, :], flat.rearrange("(r e) -> r e", e=P)).then_inc(in_loaded, 16)
                    count += 1
                return count

            sp.dma_start(cst[:, :], A["consts"]).then_inc(const_loaded, 16)
            for b in range(NB):
                sp.dma_start(x_tok[:, b, :], A["x"][0, b * P:(b + 1) * P, :]).then_inc(in_loaded, 16)
                sp.dma_start(p_tok[:, b, :], A["p_2"][0, 0, b * P:(b + 1) * P, :]).then_inc(in_loaded, 16)
            n_rows = load_rows()
            assert n_rows == IN_DMAS - 9, n_rows
            at = 0
            for name, n in (("a_A_log", 8), ("a_dt_bias", 8), ("b_sinks", 16), ("sink_2", 8)):
                sp.dma_start(bcast[:, at:at + n], A[name].to_broadcast((P, n))).then_inc(in_loaded, 16)
                at += n
            with nc.allow_non_contiguous_dma(reason="the last 16 columns of w_in"):
                sp.dma_start(ba_raw[:, :, :],
                             A["a_w_in"][0, :, 4096:4112].rearrange("(k p) n -> p k n", p=P)).then_inc(in_loaded, 16)

            for s in STAGES:
                for j in jobs_of.get(s, []):
                    {"gu": load_gated}.get(j[:2], load_wide if kind_of[j] == "wide" else load_narrow)(j)
            sp.wait_ge(out_kept, NB)
            for b in range(NB):
                sp.dma_start(out[0, b * P:(b + 1) * P, :], y_tok[:, b, :]).then_inc(out_stored, 16)
            sp.wait_ge(out_stored, 16 * NB)

        @block.tensor
        def _(pe):
            def three(o, hi, lo, mh, ml, start, stop):
                pe.matmul(o, hi, mh, start=start, stop=False)
                pe.matmul(o, hi, ml, start=False, stop=False)
                return pe.matmul(o, lo, mh, start=False, stop=stop)

            def narrow(job):
                p0, f0 = PIECE_OF[job], FILL_OF[job]
                h0 = h_before(stage_of[job])

                def chunk(j, turn, first=False):
                    pair = (f0 + j) % 2
                    pe.wait_ge(dense_drained, f0 + j + 1 + 2 * turn)
                    for r in range(2):
                        p = p0 + 2 * j + r
                        pe.wait_ge(lo_ready, p + 1 + 4 * turn)
                        for k in range(4):
                            kt = 4 * r + k
                            if first and kt % 2 == 0:
                                pe.wait_ge(h_ready, h0 + kt // 2 + 1)
                            for nt in range(4):
                                def part(w):
                                    return w[:, p % 2, 512 * k + P * nt:512 * k + P * nt + P]
                                o = D_ps[:, 2 * pair + nt // 2, T * (nt % 2):T * (nt % 2) + T]
                                last = three(o, part(w_hi), part(w_lo), h_hi[:, kt, :], h_lo[:, kt, :],
                                             start=kt == 0 and nt % 2 == 0, stop=kt == KD - 1 and nt % 2 == 1)
                        if r == 0:
                            last.then_inc(piece_used, 1)
                            if first and stage_of[job] in LATE_SCALE:
                                norm(stage_of[job])
                    last.then_inc(piece_used, 1)

                return chunk

            def run_narrow(job):
                n = COUNT_OF[job]
                chunk = narrow(job)
                for c in range(2):
                    chunk(c, 0, first=c == 0)
                done = 2

                def turn(t):
                    chunk(done, t)
                    chunk(done + 1, t)
                repeat(pe, (n - done) // 2, turn)
                for c in range(done + (n - done) // 2 * 2, n):
                    chunk(c, 0)

            def wide(job, mh, ml, ready=None):
                p0, f0, n = PIECE_OF[job], FILL_OF[job], COUNT_OF[job]
                pe.wait_ge(dense_drained, f0 + 2)
                for r in range(n):
                    p = p0 + r
                    pe.wait_ge(lo_ready, p + 1)
                    if ready:
                        pe.wait_ge(ready[0], ready[1] + r + 1)
                    final = r == n - 1
                    order = [(k, nt) for k in range(2) for nt in range(8)]
                    if final:
                        order = [(k, nt) for nt in range(8) for k in range(2)]
                    for k, nt in order:
                        kt = 2 * r + k
                        pair = (f0 + nt // 4) % 2
                        o = D_ps[:, 2 * pair + nt % 4 // 2, T * (nt % 2):T * (nt % 2) + T]
                        w0 = 1024 * k + P * nt
                        last = three(o, w_hi[:, p % 2, w0:w0 + P], w_lo[:, p % 2, w0:w0 + P],
                                     mh[:, kt, :], ml[:, kt, :],
                                     start=kt == 0 and nt % 2 == 0, stop=kt == 2 * n - 1 and nt % 2 == 1)
                        if final and k == 1 and nt == 3:
                            last.then_inc(half_filled, 1)
                    last.then_inc(piece_used, 1)

            def norm(stage):
                pe.wait_ge(sq_summed, NORM[stage] + 1)
                pe.matmul(M_ps[:, 0, 0:T], ones, sq[:, 0, :], start=True, stop=True).then_inc(ss_ready, 1)

            pe.wait_ge(const_loaded, 16)
            pe.wait_ge(in_loaded, 16 * IN_DMAS)
            for b in range(NB):
                for k in range(KD):
                    bank = M_ps if k < 4 else D_ps
                    last = pe.transpose(bank[:, k % 4, P * b:P * b + P], x_tok[:, b, P * k:P * k + P], ident)
            last.then_inc(start_turned, 1)
            for b in range(NB):
                for k in range(2):
                    pe.transpose(D_ps[:, k, T + P * b:T + P * b + P], p_tok[:, b, P * k:P * k + P], ident)
            for i, n in enumerate((N_ROWS_A, N_ROWS_B)):
                last = pe.transpose(D_ps[:, 2 + i, T:T + n], rows[0:n, i, :], ident[0:n, 0:n])
            last.then_inc(start_turned, 1)
            for s in STAGES[1:-1]:
                if s not in LATE_SCALE and s != "ple":
                    norm(s)
                if s in ("ffn0", "ffn1", "ffn2", "ffn3", "ffn4"):
                    up, down = jobs_of[s]
                    run_narrow(up)
                    wide(down, g_hi, g_lo, (g_ready, chunk_of[up]))
                elif s == "mixer_a":
                    mixer_a_pe(pe, run_narrow, wide)
                elif s == "mixer_b":
                    mixer_b_pe(pe, run_narrow, wide)
                elif s == "hybrid":
                    hybrid_pe(pe, run_narrow, wide)
                elif s == "ple":
                    wide("ple", p_hi, p_lo)
                    norm(s)
                    wide("ple_gate", h_hi, h_lo, (h_ready, h_before("ple")))
            pe.wait_ge(x_final, 2)
            for b in range(NB):
                for k in range(KD):
                    last = pe.transpose(M_ps[:, (k // 4) + 2 * b, P * (k % 4):P * (k % 4) + P],
                                        xT[:, k, P * b:P * b + P], ident)
                last.then_inc(out_turned, 1)

        @block.gpsimd
        def _(pool):
            pool.wait_ge(const_loaded, 16)
            pool.wait_ge(mask_loaded, 16)
            pool.tensor_copy(msk[:, :], mask_f32[:, :]).then_inc(mask_kept, 1)
            for s in STAGES[1:-1]:
                n = NORM[s]
                for half in range(2):
                    pool.wait_ge(sq_ready, 2 * n + half + 1)
                    k = 4 * half
                    pool.tensor_tensor(sq[:, k:k + 2, :], sq[:, k:k + 2, :], sq[:, k + 2:k + 4, :],
                                       ALU.add).then_inc(sq_folded, 1)
                    pool.wait_ge(sq_folded, 5 * n + 2 * half + 1)
                    pool.tensor_tensor(sq[:, k, :], sq[:, k, :], sq[:, k + 1, :], ALU.add).then_inc(sq_folded, 1)
                pool.wait_ge(sq_folded, 5 * n + 4)
                pool.tensor_tensor(sq[:, 0, :], sq[:, 0, :], sq[:, 4, :], ALU.add).then_inc(sq_summed, 1)
                pool.wait_ge(sq_summed, n + 1)
                pool.nop().then_inc(sq_folded, 1)
                if s == "mixer_a":
                    mixer_a_pool(pool)
                elif s == "hybrid":
                    hybrid_pool(pool)

        @block.scalar
        def _(act):
            link = Chain(act, sem("act_chain"))
            ahead = [0]

            def split_hi(turn=0, q=0):
                p = ahead[0] + q
                if p >= n_pieces:
                    return
                act.wait_ge(raw_loaded[p % RAW_SLOTS], 32 * (p // RAW_SLOTS + 1 + turn))
                if p >= SPLIT_SLOTS:
                    act.wait_ge(piece_used, p - SPLIT_SLOTS + 1 + 4 * turn)
                if p in HEAD_PIECES:
                    assert isinstance(turn, int)
                    for k in range(4):
                        last = act.activation(as_heads(w_hi, p % 2, k), by_heads(raw, p % RAW_SLOTS, k), ACT.Copy)
                    last.then_inc(hi_ready, 1)
                    return
                act.activation(w_hi[:, p % 2, :], raw[:, p % RAW_SLOTS, :], ACT.Copy).then_inc(hi_ready, 1)

            def splits(n):
                n = min(n, n_pieces - ahead[0])

                def turn(t):
                    for q in range(4):
                        split_hi(t, q)
                repeat(act, n // 4, turn)
                ahead[0] += n // 4 * 4
                for _ in range(n % 4):
                    split_hi()
                    ahead[0] += 1

            def narrow(job, body, links=0, first=0, n=None):
                n, p0 = n or COUNT_OF[job], PIECE_OF[job] + 2 * first

                def turn(t):
                    for q in range(2):
                        split_hi(t, 2 * q)
                        split_hi(t, 2 * q + 1)
                        act.wait_ge(piece_used, p0 + 2 * q + 2 + 4 * t)
                        body(2 * t + q, q)
                repeat(act, n // 2, turn, link, links)
                ahead[0] += n // 2 * 4
                if n % 2:
                    split_hi(0, 0)
                    split_hi(0, 1)
                    ahead[0] += 2
                    act.wait_ge(piece_used, p0 + 2 * n)
                    body(n - 1, (n - 1) % 2)

            def norm(stage):
                n = NORM[stage]
                fill = fill_before(stage)
                for half in range(2):
                    if fill is None:
                        act.wait_ge(x_ready, x_ready_at(stage))
                    else:
                        act.wait_ge(dense_drained, 2 + fill + half + 1)
                    act.activation(sq[:, 4 * half:4 * half + 4, :], xT[:, 4 * half:4 * half + 4, :],
                                   ACT.Square).then_inc(sq_ready, 1)
                    if half == 0 and stage in BEFORE:
                        splits(1)
                act.preload_act_table_set(LN_EXP)
                act.wait_ge(ss_ready, n + 1)
                link(act.activation(rstd[:, :], M_ps[:, 0, 0:T], ACT.Ln, bias=eps_col, scale=1.0 / D))
                act.activation(rstd[:, :], rstd[:, :], ACT.Exp, scale=-0.5).then_inc(rstd_ready, 1)

            act.wait_ge(const_loaded, 16)
            splits(2)
            for s in STAGES[1:-1]:
                norm(s)
                if s in ("ffn0", "ffn1", "ffn2", "ffn3", "ffn4"):
                    up, down = jobs_of[s]
                    f0 = FILL_OF[up]

                    def body(c, q):
                        act.wait_ge(gate_scaled, chunk_of[up] + c + 1)
                        act.activation(act2[:, q, :, :], act2[:, q, :, :], ACT.Silu).then_inc(act_ready, 1)

                    def body_relu(c, q):
                        act.wait_ge(dense_drained, 2 + f0 + c)
                        for b in range(2):
                            act.activation(act2[:, b, :, :],
                                           D_ps[:, 2 * ((f0 + q) % 2) + b, :].rearrange("p (k t) -> p k t", t=T),
                                           ACT.Relu).then_inc(act_ready, 1)
                    act.preload_act_table(ACT.Silu)
                    narrow(up, body if up != "ff1" else body_relu)
                    splits(pieces_of[down] - 1)
                elif s == "mixer_a":
                    mixer_a_act(act, link, narrow, splits)
                elif s == "mixer_b":
                    mixer_b_act(act, link, narrow, splits)
                elif s == "hybrid":
                    hybrid_act(act, link, narrow, splits)
                elif s == "ple":
                    ple_act(act, link, splits)
            for b in range(NB):
                act.wait_ge(out_turned, b + 1)
                act.activation(y_tok[:, b, :], M_ps[:, 2 * b:2 * b + 2, :].rearrange("p a n -> p (a n)"),
                               ACT.Copy).then_inc(out_kept, 1)

        @block.vector
        def _(dve):
            link = Chain(dve, sem("dve_chain"))
            ahead = [0]

            def split_lo(turn=0, q=0):
                p = ahead[0] + q
                if p >= n_pieces:
                    return
                dve.wait_ge(hi_ready, p + 1 + 4 * turn)
                if p in HEAD_PIECES:
                    for k in range(4):
                        last = dve.tensor_tensor(as_heads(w_lo, p % 2, k), by_heads(raw, p % RAW_SLOTS, k),
                                                 as_heads(w_hi, p % 2, k).bitcast(F32), ALU.subtract)
                    last.then_inc(lo_ready, 1)
                    return
                dve.tensor_tensor(w_lo[:, p % 2, :], raw[:, p % RAW_SLOTS, :], w_hi[:, p % 2, :].bitcast(F32),
                                  ALU.subtract).then_inc(lo_ready, 1)

            def splits(n):
                n = min(n, n_pieces - ahead[0])

                def turn(t):
                    for q in range(4):
                        split_lo(t, q)
                repeat(dve, n // 4, turn)
                ahead[0] += n // 4 * 4
                for _ in range(n % 4):
                    split_lo()
                    ahead[0] += 1

            def narrow(job, body, links=0, first=0, n=None):
                n, p0 = n or COUNT_OF[job], PIECE_OF[job] + 2 * first

                def turn(t):
                    for q in range(2):
                        split_lo(t, 2 * q)
                        split_lo(t, 2 * q + 1)
                        dve.wait_ge(piece_used, p0 + 2 * q + 2 + 4 * t)
                        body(2 * t + q, q)
                repeat(dve, n // 2, turn, link, 2 * links)
                ahead[0] += n // 2 * 4
                if n % 2:
                    split_lo(0, 0)
                    split_lo(0, 1)
                    ahead[0] += 2
                    dve.wait_ge(piece_used, p0 + 2 * n)
                    body(n - 1, (n - 1) % 2)

            def split_act(full, hi, lo):
                link(dve.tensor_copy(hi, full))
                return dve.tensor_tensor(lo, full, hi.bitcast(F32), ALU.subtract)

            def times_w(stage, halves=(0, 1)):
                name, c0 = NORM_COL[stage]
                for j in [2 * e + i for e in halves for i in range(2)]:
                    for k in (2 * j, 2 * j + 1):
                        last = dve.tensor_scalar(full3[:, j % 3, k % 2, :], xT[:, k, :], column(name, c0 + k), None,
                                                 ALU.mult)
                    link(last)
                    split_act(full3[:, j % 3, :, :], h_hi[:, 2 * j:2 * j + 2, :],
                              h_lo[:, 2 * j:2 * j + 2, :]).then_inc(h_ready, 1)

            def norm(stage, to_h=True):
                n = NORM[stage]
                name, c0 = NORM_COL[stage]
                dve.wait_ge(rstd_ready, n + 1)
                if stage in LATE_SCALE:
                    return
                if not to_h:
                    for k in range(KD):
                        last = dve.scalar_tensor_tensor(out=xT[:, k, :], in0=xT[:, k, :], scalar=column(name, c0 + k),
                                                        in1=rstd[:, :], op0=ALU.mult, op1=ALU.mult)
                    last.then_inc(x_ready, 1)
                    dve.wait_ge(x_ready, x_ready_at("hybrid"))
                    return
                for j in range(6):
                    last = None
                    if j >= 2:
                        i = j - 2
                        dve.tensor_tensor(h_lo[:, 2 * i:2 * i + 2, :], full3[:, i % 3, :, :],
                                          h_hi[:, 2 * i:2 * i + 2, :].bitcast(F32),
                                          ALU.subtract).then_inc(h_ready, 1)
                    if j < 4:
                        for k in (2 * j, 2 * j + 1):
                            last = dve.scalar_tensor_tensor(out=full3[:, j % 3, k % 2, :], in0=xT[:, k, :],
                                                            scalar=column(name, c0 + k), in1=rstd[:, :],
                                                            op0=ALU.mult, op1=ALU.mult)
                    if 1 <= j < 5:
                        i = j - 1
                        last = dve.tensor_copy(h_hi[:, 2 * i:2 * i + 2, :], full3[:, i % 3, :, :])
                    if last is not None:
                        link(last)

            def before_norm(stage, e):
                dve.wait_ge(dense_drained, 2 + fill_before(stage) + e + 1)
                times_w(stage, (e,))

            def next_stage(s):
                return STAGES[STAGES.index(s) + 1]

            def residual(job, scale):
                f0 = FILL_OF[job]
                for e in range(2):
                    pair = 2 * ((f0 + e) % 2)
                    wait_half(dve, job, e)
                    x2 = xT[:, 4 * e:4 * e + 4, :].rearrange("p k t -> p (k t)")
                    dve.scalar_tensor_tensor(out=x2, in0=D_ps[:, pair:pair + 2, :].rearrange("p a n -> p (a n)"),
                                             scalar=scale, in1=x2, op0=ALU.mult, op1=ALU.add).then_inc(dense_drained, 1)
                    if next_stage(stage_of[job]) in LATE_SCALE:
                        before_norm(next_stage(stage_of[job]), e)
                splits(1)

            dve.wait_ge(start_turned, 2)
            for half, bank in enumerate((M_ps, D_ps)):
                last = dve.tensor_copy(xT[:, 4 * half:4 * half + 4, :], bank[:, :, 0:T])
            last.then_inc(x_ready, 1)
            link(dve.tensor_copy(cols[:, 0:N_ROWS_A], D_ps[:, 2, T:T + N_ROWS_A]))
            link(dve.tensor_copy(cols[:, P:P + N_ROWS_B], D_ps[:, 3, T:T + N_ROWS_B]))
            link(dve.tensor_copy(full3[:, 0, :, :], D_ps[:, 0:2, T:2 * T]))
            split_act(full3[:, 0, :, :], p_hi[:, :, :], p_lo[:, :, :]).then_inc(dense_drained, 2)
            dve.wait_ge(dense_drained, 2)
            if "ffn0" in LATE_SCALE:
                dve.wait_ge(x_ready, 1)
                times_w("ffn0")
            splits(2)
            for s in STAGES[1:-1]:
                if s != "ple":
                    norm(s, s != "final_norm")
                if s == "ffn0":
                    dve.wait_ge(mask_kept, 1)
                if s in ("ffn0", "ffn1", "ffn2", "ffn3", "ffn4"):
                    up, down = jobs_of[s]
                    f0, c0 = FILL_OF[up], chunk_of[up]

                    def by_rms(n):
                        return over_mid(rstd[:, :], n)

                    def body(c, q):
                        lower, upper = (D_ps[:, 2 * ((f0 + q) % 2) + i, :].rearrange("p (k t) -> p k t", t=T)
                                        for i in range(2))
                        dve.tensor_tensor(act2[:, q, :, :], lower, by_rms(2), ALU.mult).then_inc(gate_scaled, 1)
                        dve.tensor_tensor(full2[:, q, :, :], upper, by_rms(2), ALU.mult).then_inc(dense_drained, 1)
                        dve.wait_ge(dense_drained, 2 + f0 + c + 1)
                        dve.wait_ge(act_ready, chunk_of[up] + c + 1)
                        link(dve.tensor_tensor(full2[:, q, :, :], act2[:, q, :, :], full2[:, q, :, :], ALU.mult))
                        k = bass.ds(2 * c, 2)
                        split_act(full2[:, q, :, :], g_hi[:, k, :], g_lo[:, k, :]).then_inc(g_ready, 1)

                    def body_square(c, q):
                        for b in range(2):
                            dve.wait_ge(act_ready, chunk_of[up] + 2 * c + b + 1)
                            link(dve.tensor_tensor(full2[:, b, :, :], act2[:, b, :, :], by_rms(2), ALU.mult))
                            ins = dve.tensor_tensor(full2[:, b, :, :], full2[:, b, :, :], full2[:, b, :, :], ALU.mult)
                            if b:
                                ins.then_inc(dense_drained, 1)
                                dve.wait_ge(dense_drained, 2 + f0 + c + 1)
                            else:
                                link(ins)
                            k = bass.ds(4 * c + 2 * b, 2)
                            split_act(full2[:, b, :, :], g_hi[:, k, :], g_lo[:, k, :]).then_inc(g_ready, 1)
                    if up == "ff1":
                        narrow(up, body_square, 5)
                    else:
                        narrow(up, body, 2)
                    splits(pieces_of[down] - 1)
                    residual(down, 1.0 if up == "ff1" else 0.5)
                elif s == "mixer_a":
                    mixer_a_dve(dve, link, narrow, splits, split_act)
                    residual("a_out", 1.0)
                elif s == "mixer_b":
                    mixer_b_dve(dve, link, narrow, splits, split_act, before_norm)
                elif s == "hybrid":
                    hybrid_dve(dve, link, narrow, splits, split_act)
                    residual("out2", 1.0)
                elif s == "ple":
                    ple_dve(dve, link, splits, norm)
            if STAGES[-2] != "ple":
                dve.wait_ge(dense_drained, 2 + FILL_OF[jobs[-1]] + 2)
                dve.nop().then_inc(x_final, 2)


_INS = ["x", "ffn1_norm", "ffn1_w_gu", "ffn1_w_down", "mix_norm", "ffn2_norm", "ffn2_w_gu", "ffn2_w_down",
        "a_w_in", "a_w_conv", "a_A_log", "a_dt_bias", "a_out_norm", "a_w_out", "b_w_in", "b_b_in", "b_sinks",
        "b_w_out", "b_b_out", "final_norm", "p_2", "norm_mix_2", "w_in_2", "shift_mu_2", "q_norm_2", "k_norm_2",
        "sink_2", "w0_2", "w2_2", "a0_2", "a2_2", "g2_2", "k_k_2", "k_a_2", "r_k_2", "lnx_w_2", "lnx_b_2",
        "w_up_attn_2", "w_up_rwkv_2", "w_out_2", "norm_ffn_2", "w_ff1_2", "w_ff2_2", "norm_ple_2",
        "w_ple_gate_2", "w_ple_2"]


def kernel(**inputs):
    import concourse.bacc as bacc
    from concourse.bass_utils import run_bass_kernel_spmd

    nc = bacc.Bacc("TRN2", target_bir_lowering=False, num_devices=1)
    arrays = {f"in_{n}": np.ascontiguousarray(inputs[n]) for n in _INS}
    arrays["in_consts"], arrays["in_masks"] = constants()
    A = {k[3:]: nc.dram_tensor(k, a.shape, mybir.dt.from_np(a.dtype), kind="ExternalInput").ap()
         for k, a in arrays.items()}
    out = nc.dram_tensor("out_0", (1, T, D), F32, kind="ExternalOutput").ap()
    build(nc, A, out)
    r = run_bass_kernel_spmd(nc, [arrays], core_ids=[0])
    return r.results[0]["out_0"]
```
